# Optimizing a Trainium2 kernel written in Bass

```python
import jax, jax.numpy as jnp
from jax import lax
import numpy as np

D_MODEL = 2048
BATCH = 1
SEQ = 256
DEPTH = 2

PLE_DIM = 256
RET_WIDTH = D_MODEL // 2
RET_HEADS = 4
RET_HEAD_DIM = RET_WIDTH // RET_HEADS
RET_CHUNK = 128
RET_ROT_BASE = 10000.0
ATT_HEAD_DIM = 64
ATT_WIDTH = D_MODEL - RET_WIDTH
ATT_HEADS = ATT_WIDTH // ATT_HEAD_DIM
ATT_KV_HEADS = ATT_HEADS // 8
KV_WIDTH = ATT_KV_HEADS * ATT_HEAD_DIM
WINDOW = 128
ROPE_THETA = 10000.0
MIX_WIDTH = RET_WIDTH + ATT_WIDTH
SPLIT_SIZES = [RET_WIDTH, RET_WIDTH, RET_WIDTH, RET_WIDTH, ATT_WIDTH, KV_WIDTH, KV_WIDTH]
IN_WIDTH = sum(SPLIT_SIZES)
SPLIT_POINTS = np.cumsum(SPLIT_SIZES)[:-1].tolist()
D_FF = 5632
CONV_WIDTH = 3
LN_EPS = 1e-5
GN_EPS = 1e-6
DEEPNORM_ALPHA = (2 * DEPTH) ** 0.25
DEEPNORM_BETA = (8 * DEPTH) ** -0.25

kernel_name = "hybrid_retention_swa_sink_deepnorm"

F32 = jnp.float32

def layer_norm(x, g, b):
    xf = x.astype(F32)
    mu = xf.mean(-1, keepdims=True)
    var = jnp.square(xf - mu).mean(-1, keepdims=True)
    y = (xf - mu) * lax.rsqrt(var + LN_EPS) * g.astype(F32) + b.astype(F32)
    return y.astype(x.dtype)

def rotary(x, positions, inv_freq):
    ang = positions.astype(F32)[..., None] * inv_freq
    cos = jnp.cos(ang)[:, :, None, :]
    sin = jnp.sin(ang)[:, :, None, :]
    x1, x2 = jnp.split(x.astype(F32), 2, axis=-1)
    return jnp.concatenate([x1 * cos - x2 * sin, x1 * sin + x2 * cos], axis=-1).astype(x.dtype)

def retention_chunkwise(q, k, v):
    B, S, H, dk = q.shape
    dv = v.shape[-1]
    C = RET_CHUNK
    N = S // C
    log_g = jnp.log1p(-jnp.exp2(-5.0 - jnp.arange(H, dtype=F32)))
    q = q.astype(F32).reshape(B, N, C, H, dk)
    k = k.astype(F32).reshape(B, N, C, H, dk) * (dk ** -0.5)
    v = v.astype(F32).reshape(B, N, C, H, dv)
    idx = jnp.arange(C, dtype=F32)
    diff = idx[:, None] - idx[None, :]
    decay = jnp.where(diff[None] >= 0, jnp.exp(log_g[:, None, None] * jnp.maximum(diff, 0.0)[None]), 0.0)
    scores = jnp.einsum('bnihd,bnjhd->bnhij', q, k) * decay
    inner = jnp.einsum('bnhij,bnjhe->bnihe', scores, v)
    q_decay = jnp.exp(log_g[None, :] * (idx[:, None] + 1.0))
    k_decay = jnp.exp(log_g[None, :] * (C - 1.0 - idx[:, None]))
    chunk_decay = jnp.exp(log_g * C)

    def step(state, inp):
        qc, kc, vc = inp
        cross = jnp.einsum('bihd,bhde->bihe', qc, state) * q_decay[None, :, :, None]
        state = state * chunk_decay[None, :, None, None] + jnp.einsum(
            'bjhd,bjhe->bhde', kc * k_decay[None, :, :, None], vc)
        return state, cross

    init = jnp.zeros((B, H, dk, dv), F32)
    _, cross = lax.scan(step, init, (jnp.moveaxis(q, 1, 0), jnp.moveaxis(k, 1, 0), jnp.moveaxis(v, 1, 0)))
    cross = jnp.moveaxis(cross, 0, 1)
    return (inner + cross).reshape(B, S, H, dv)

def head_group_norm(y, g, b):
    mu = y.mean(-1, keepdims=True)
    var = jnp.square(y - mu).mean(-1, keepdims=True)
    y = (y - mu) * lax.rsqrt(var + GN_EPS)
    B, S, H, dv = y.shape
    return y.reshape(B, S, H * dv) * g.astype(F32) + b.astype(F32)

def sliding_window_attention_sinks(q, k, v, sinks):
    B, S, Hq, d = q.shape
    Hkv = k.shape[2]
    G = Hq // Hkv
    W = WINDOW
    N = S // W
    qb = q.astype(F32).reshape(B, N, W, Hkv, G, d)

    def band(t):
        t = t.astype(F32)
        prev = jnp.pad(t, ((0, 0), (W, 0), (0, 0), (0, 0)))[:, :S].reshape(B, N, W, Hkv, d)
        return jnp.concatenate([prev, t.reshape(B, N, W, Hkv, d)], axis=2)

    kb = band(k)
    vb = band(v)
    blk = jnp.arange(N)[:, None, None]
    qi = jnp.arange(W)[None, :, None]
    kj = jnp.arange(2 * W)[None, None, :]
    delta = qi + W - kj
    mask = (delta >= 0) & (delta < W) & (blk * W - W + kj >= 0)
    s = jnp.einsum('bnihgd,bnjhd->bnhgij', qb, kb) * (d ** -0.5)
    s = jnp.where(mask[None, :, None, None], s, -jnp.inf)
    sink = sinks.astype(F32).reshape(Hkv, G)[None, None, :, :, None, None]
    m = jnp.maximum(s.max(-1, keepdims=True), sink)
    pr = jnp.exp(s - m)
    pr = pr / (pr.sum(-1, keepdims=True) + jnp.exp(sink - m))
    o = jnp.einsum('bnhgij,bnjhd->bnihgd', pr, vb)
    return o.reshape(B, S, Hq * d)

def causal_depthwise_conv(h, w, b):
    S = h.shape[1]
    hp = jnp.pad(h, ((0, 0), (CONV_WIDTH - 1, 0), (0, 0)))
    out = b
    for kk in range(CONV_WIDTH):
        out = out + hp[:, kk:kk + S] * w[kk]
    return out

def setup_inputs(seed: int = 0) -> dict:
    key = jax.random.key(seed)
    ks = jax.random.split(key, 20)
    nrm = jax.random.normal
    beta = DEEPNORM_BETA
    x = nrm(ks[0], (BATCH, SEQ, D_MODEL), F32)
    p = nrm(ks[1], (DEPTH, BATCH, SEQ, PLE_DIM), F32)
    positions = jnp.broadcast_to(jnp.arange(SEQ, dtype=jnp.int32)[None, :], (BATCH, SEQ))
    col_scale = jnp.concatenate([
        jnp.ones((2 * RET_WIDTH,), F32), jnp.full((RET_WIDTH,), beta, F32), jnp.ones((RET_WIDTH,), F32),
        jnp.ones((ATT_WIDTH + KV_WIDTH,), F32), jnp.full((KV_WIDTH,), beta, F32)])
    w_in = nrm(ks[2], (DEPTH, D_MODEL, IN_WIDTH), F32) * (D_MODEL ** -0.5) * col_scale
    w_out = nrm(ks[3], (DEPTH, MIX_WIDTH, D_MODEL), F32) * (MIX_WIDTH ** -0.5) * beta
    ret_norm_g = 1.0 + 0.02 * nrm(ks[4], (DEPTH, RET_WIDTH), F32)
    ret_norm_b = 0.02 * nrm(ks[5], (DEPTH, RET_WIDTH), F32)
    attn_sinks = nrm(ks[6], (DEPTH, ATT_HEADS), F32)
    ln1_g = 1.0 + 0.02 * nrm(ks[7], (DEPTH, D_MODEL), F32)
    ln1_b = 0.02 * nrm(ks[8], (DEPTH, D_MODEL), F32)
    w_ffn_up = nrm(ks[9], (DEPTH, D_MODEL, 2 * D_FF), F32) * (D_MODEL ** -0.5) * beta
    ffn_conv_w = nrm(ks[10], (DEPTH, CONV_WIDTH, 2 * D_FF), F32) * (CONV_WIDTH ** -0.5)
    ffn_conv_b = 0.02 * nrm(ks[11], (DEPTH, 2 * D_FF), F32)
    w_ffn_down = nrm(ks[12], (DEPTH, D_FF, D_MODEL), F32) * (D_FF ** -0.5) * beta
    ln2_g = 1.0 + 0.02 * nrm(ks[13], (DEPTH, D_MODEL), F32)
    ln2_b = 0.02 * nrm(ks[14], (DEPTH, D_MODEL), F32)
    w_ple_gate = nrm(ks[15], (DEPTH, D_MODEL, D_MODEL), F32) * (D_MODEL ** -0.5)
    b_ple_gate = 0.01 * nrm(ks[16], (DEPTH, D_MODEL), F32)
    w_ple_proj = nrm(ks[17], (DEPTH, PLE_DIM, D_MODEL), F32) * (PLE_DIM ** -0.5) * beta
    return {"x": x, "p": p, "positions": positions, "w_in": w_in, "w_out": w_out,
            "ret_norm_g": ret_norm_g, "ret_norm_b": ret_norm_b, "attn_sinks": attn_sinks,
            "ln1_g": ln1_g, "ln1_b": ln1_b, "w_ffn_up": w_ffn_up, "ffn_conv_w": ffn_conv_w,
            "ffn_conv_b": ffn_conv_b, "w_ffn_down": w_ffn_down, "ln2_g": ln2_g, "ln2_b": ln2_b,
            "w_ple_gate": w_ple_gate, "b_ple_gate": b_ple_gate, "w_ple_proj": w_ple_proj}

def reference(x, p, positions, w_in, w_out, ret_norm_g, ret_norm_b, attn_sinks, ln1_g, ln1_b,
              w_ffn_up, ffn_conv_w, ffn_conv_b, w_ffn_down, ln2_g, ln2_b, w_ple_gate, b_ple_gate,
              w_ple_proj):
    B, S, _ = x.shape
    ret_inv_freq = 1.0 / (RET_ROT_BASE ** jnp.linspace(0.0, 1.0, RET_HEAD_DIM // 2, dtype=F32))
    att_inv_freq = ROPE_THETA ** (-jnp.arange(0, ATT_HEAD_DIM, 2, dtype=F32) / ATT_HEAD_DIM)
    for i in range(DEPTH):
        proj = x @ w_in[i]
        rq, rk, rv, rg, aq, ak, av = jnp.split(proj, SPLIT_POINTS, axis=-1)
        rq = rotary(rq.reshape(B, S, RET_HEADS, RET_HEAD_DIM), positions, ret_inv_freq)
        rk = rotary(rk.reshape(B, S, RET_HEADS, RET_HEAD_DIM), positions, ret_inv_freq)
        ret = retention_chunkwise(rq, rk, rv.reshape(B, S, RET_HEADS, RET_HEAD_DIM))
        ret = jax.nn.silu(rg.astype(F32)) * head_group_norm(ret, ret_norm_g[i], ret_norm_b[i])
        aq = rotary(aq.reshape(B, S, ATT_HEADS, ATT_HEAD_DIM), positions, att_inv_freq)
        ak = rotary(ak.reshape(B, S, ATT_KV_HEADS, ATT_HEAD_DIM), positions, att_inv_freq)
        att = sliding_window_attention_sinks(aq, ak, av.reshape(B, S, ATT_KV_HEADS, ATT_HEAD_DIM),
                                             attn_sinks[i])
        mix = jnp.concatenate([ret, att], axis=-1).astype(x.dtype) @ w_out[i]
        x = layer_norm(DEEPNORM_ALPHA * x + mix, ln1_g[i], ln1_b[i])
        h = causal_depthwise_conv(x @ w_ffn_up[i], ffn_conv_w[i], ffn_conv_b[i])
        gate, up = jnp.split(h, 2, axis=-1)
        ffn = (jax.nn.silu(gate) * up) @ w_ffn_down[i]
        ple = (p[i] @ w_ple_proj[i]) * jax.nn.sigmoid(x @ w_ple_gate[i] + b_ple_gate[i])
        x = layer_norm(DEEPNORM_ALPHA * x + ffn + ple, ln2_g[i], ln2_b[i])
    return x


_drawn_inputs = setup_inputs


def setup_inputs(seed=0):
    import zlib

    import numpy as np

    out = dict(_drawn_inputs(seed))
    spreads = {}
    factors = {'ret_norm_g': 8.0,
     'ret_norm_b': 8.0,
     'attn_sinks': 25.517,
     'ffn_conv_b': 8.0,
     'b_ple_gate': 40.822}
    for name, (base, spread) in spreads.items():
        noise = np.random.default_rng([zlib.crc32(name.encode()), seed]).standard_normal(out[name].shape)
        drawn = base * np.exp(spread * noise) if base else spread * noise
        out[name] = __import__('jax').numpy.asarray(drawn.astype(out[name].dtype))
    for name, factor in factors.items():
        out[name] = (out[name] * factor).astype(out[name].dtype)
    return out
```

```python
from contextlib import ExitStack, contextmanager

import numpy as np
import concourse.bass as bass
from concourse import mybir

F32 = mybir.dt.float32
F32R = mybir.dt.float32r
I32 = mybir.dt.int32
ALU = mybir.AluOpType
ACT = mybir.ActivationFunctionType
AX_X = mybir.AxisListType.X

P = 128
D_MODEL, SEQ, DEPTH, PLE_DIM = 2048, 256, 2, 256
D_FF = 5632
M = SEQ // P
KD = D_MODEL // P
RET_HEADS, RET_DIM = 4, 256
RET_WIDTH = RET_HEADS * RET_DIM
ATT_HEADS, ATT_KV, ATT_DIM = 16, 2, 64
ATT_WIDTH = ATT_HEADS * ATT_DIM
RQ, RK, RV, RG, AQ = (n * RET_WIDTH for n in range(5))
AK = AQ + ATT_WIDTH
AV = AK + ATT_KV * ATT_DIM
IN_WIDTH = AV + ATT_KV * ATT_DIM
FREQS = RET_DIM // 2 + ATT_DIM // 2
ALPHA = float((2 * DEPTH) ** 0.25)
LN_EPS, GN_EPS = 1e-5, 1e-6
MASKED = -3.0e38

PANEL = 2048
RAW_SLOTS, SPLIT_SLOTS = 4, 2
BANK = 512
FF_GROUP = 4
FF_GROUPS = D_FF // P // FF_GROUP
KFF = D_FF // P

KV_PANELS = 2
IN_LOOPS, IN_BODY = AK // 1024, 8
OUT_PANELS = KD
PLE_PANELS = PLE_DIM // P
UP_BODY = 8
GATE_PANELS = KD
KV_AT = 0
IN_AT = KV_AT + KV_PANELS
OUT_AT = IN_AT + IN_LOOPS * IN_BODY
PLE_AT = OUT_AT + OUT_PANELS
UP_AT = PLE_AT + PLE_PANELS
GATE_AT = UP_AT + FF_GROUPS * UP_BODY
DOWN_AT = GATE_AT + GATE_PANELS
PANELS = DOWN_AT + KFF

COPIES = 2 * (1 + 2 * IN_LOOPS)
XT_BANKS = KD // 2
T_BANKS = 2 * XT_BANKS + 1
QK_BANKS = 4 + 1 + 4 + 4
UNITS = M * ATT_KV * 2
EVACS = 3 * 8 + 0


def layered(l, per_layer, n):
    return l * per_layer + n


class Chain:

    def __init__(self, eng, sem):
        self.eng, self.sem, self.base, self.n = eng, sem, 0, 0

    def __call__(self, instruction):
        instruction.then_inc(self.sem, 1)
        self.n += 1
        self.eng.wait_ge(self.sem, self.base + self.n)

    @contextmanager
    def loop(self, count, links):
        base, first = self.base, self.n
        with self.eng.Fori(0, count) as i:
            self.base = base + i * links
            yield i
            assert self.n - first == links, (self.n - first, links)
        self.base, self.n = base, first + count * links


SCALE = 160
TWO_PI = 6283185307179586476925286766559005768394338798750 * 2 ** SCALE // 10 ** 48
PERIODS = 4096


def angle_parts(value, lowest_bits):
    parts = []
    for bit in lowest_bits:
        unit = 2 ** (SCALE + bit)
        n = (2 * value + unit) // (2 * unit)
        parts.append(float(n) * 2.0 ** bit)
        value -= n * unit
    return parts


COARSE = angle_parts(TWO_PI * PERIODS, (8, 1, -6, -13, -20, -27, -34))
FINE = angle_parts(TWO_PI, (-9, -21, -33))
ROUND = 1.5 * 2.0 ** 23


def build(nc, a, out):
    with ExitStack() as ctx:
        def sb(name, shape, dt=F32):
            return ctx.enter_context(nc.sbuf_tensor(name, shape, dt))

        def sem(name):
            return ctx.enter_context(nc.semaphore(name))

        xt = sb("xt", [P, M, D_MODEL])
        work = sb("work", [P, KFF * SEQ])
        xT_hi = sb("xT_hi", [P, KD, SEQ], F32R)
        xT_lo = sb("xT_lo", [P, KD, SEQ], F32R)
        pT_hi = sb("pT_hi", [P, PLE_PANELS, SEQ], F32R)
        pT_lo = sb("pT_lo", [P, PLE_PANELS, SEQ], F32R)
        raw = sb("raw", [P, RAW_SLOTS, PANEL])
        w_hi = sb("w_hi", [P, SPLIT_SLOTS, PANEL], F32R)
        w_lo = sb("w_lo", [P, SPLIT_SLOTS, PANEL], F32R)
        vec = sb("vec", [P, 2, D_MODEL])
        scratch = sb("scratch", [P, 6656])
        cosine = sb("cosine", [P, M, FREQS])
        sine = sb("sine", [P, M, FREQS])
        ident = sb("ident", [P, P])
        band = sb("band", [P, 2 * P])
        causal = sb("causal", [P, P])
        decay = sb("decay", [P, M, 2 * RET_HEADS])
        position = sb("position", [P, M], I32)
        position_f = sb("position_f", [P, M])
        sinks = sb("sinks", [P, ATT_HEADS])
        small = sb("small", [P, 96])

        proj = work[:, 0:M * IN_WIDTH].rearrange("p (m c) -> p m c", m=M)
        gated = work[:, :].rearrange("p (f t) -> p f t", t=SEQ)

        freq = scratch[:, 0:FREQS]
        angle = scratch[:, 320:640].rearrange("p (m f) -> p m f", m=M)
        coarse_k = scratch[:, 640:960].rearrange("p (m f) -> p m f", m=M)
        fine_k = scratch[:, 960:1280].rearrange("p (m f) -> p m f", m=M)
        p_tok = scratch[:, 0:M * PLE_DIM].rearrange("p (m c) -> p m c", m=M)
        rot_a = scratch[:, 2048:3072]
        rot_b = scratch[:, 3072:4096]
        k_twice = scratch[:, 4096:4608].rearrange("p (m k e d) -> p m k e d", m=M, k=ATT_KV, e=2)
        aqT = scratch[:, 0:2048].rearrange("p (c t) -> p c t", t=SEQ)
        akT = scratch[:, 6144:6656].rearrange("p (c t) -> p c t", t=SEQ)
        rqT = scratch[:, 2048:4096].rearrange("p (c t) -> p c t", t=SEQ)
        rkT = scratch[:, 4096:6144].rearrange("p (c t) -> p c t", t=SEQ)
        probs = [proj[:, 0, 1024 * u:1024 * (u + 1)].rearrange("p (h k) -> p h k", h=4) for u in range(2)]
        probsT = [proj[:, 1, 1024 * u:1024 * (u + 1)].rearrange("p (h k) -> p h k", h=4) for u in range(2)]
        scoresT = [proj[:, 0, 512 * u:512 * u + 384] for u in range(2)]
        ret_y = scratch[:, 0:2048].rearrange("p (m c) -> p m c", m=M)
        ret_sig = scratch[:, 2048:4096].rearrange("p (m c) -> p m c", m=M)
        ple = scratch[:, 0:4096].rearrange("p (m c) -> p m c", m=M)
        tmp = [scratch[:, 4096:5120], scratch[:, 5120:6144]]
        conv_rows = scratch[:, 4096:4608].rearrange("p (k c) -> p k c", k=4)
        conv = scratch[:, 6144:6144 + 4 * 2 * KFF].rearrange("p (k c) -> p k c", k=4)
        stats = small[:, 0:48].rearrange("p (m s) -> p m s", m=M)
        moments = small[:, 48:52].rearrange("p (m s) -> p m s", m=M)
        rstd = small[:, 52:54]
        ret_moments = small[:, 0:16].rearrange("p (m h s) -> p m h s", m=M, h=RET_HEADS)
        ret_stats = small[:, 16:22]
        ret_rstd = small[:, 24:32].rearrange("p (m h) -> p m h", m=M)
        row_max = [small[:, 54 + 4 * u:58 + 4 * u] for u in range(2)]
        neg_max = [small[:, 62 + 4 * u:66 + 4 * u] for u in range(2)]
        sink_gap = [small[:, 70 + 4 * u:74 + 4 * u] for u in range(2)]
        row_sum = [small[:, 78 + 4 * u:82 + 4 * u] for u in range(2)]
        conv_group = small[:, 0:32].rearrange("p (k h c) -> p k h c", k=4, h=2)

        ps = ctx.enter_context(nc.psum_tensor("ps", [P, 8, BANK], F32))

        raw_arrived = [sem(f"raw_arrived{s}") for s in range(RAW_SLOTS)]
        hi_split = sem("hi_split")
        panels_split = sem("panels_split")
        panels_used = sem("panels_used")
        x_loaded = sem("x_loaded")
        consts_loaded = sem("consts_loaded")
        freq_loaded = sem("freq_loaded")
        p_loaded = sem("p_loaded")
        sinks_loaded = sem("sinks_loaded")
        ret_vec_loaded = sem("ret_vec_loaded")
        ln_vec_loaded = sem("ln_vec_loaded")
        ple_vec_loaded = sem("ple_vec_loaded")
        conv_loaded = sem("conv_loaded")
        stored = sem("stored")
        angles_reduced = sem("angles_reduced")
        tables_made = sem("tables_made")
        x_normed = sem("x_normed")
        transposed = sem("transposed")
        xT_hi_done = sem("xT_hi_done")
        xT_lo_done = sem("xT_lo_done")
        proj_copied = sem("proj_copied")
        rotated = sem("rotated")
        qk_transposed = sem("qk_transposed")
        qk_copied = sem("qk_copied")
        scores_done = sem("scores_done")
        max_done = sem("max_done")
        exp_done = sem("exp_done")
        probs_done = sem("probs_done")
        probsT_done = sem("probsT_done")
        probsT_copied = sem("probsT_copied")
        att_done = sem("att_done")
        att_hi = sem("att_hi")
        att_lo = sem("att_lo")
        ret_scores_done = sem("ret_scores_done")
        ret_cross_copied = sem("ret_cross_copied")
        ret_scores_masked = sem("ret_scores_masked")
        ret_done = sem("ret_done")
        ret_copied = sem("ret_copied")
        ret_var = sem("ret_var")
        ret_std = sem("ret_std")
        ret_sigmoid = sem("ret_sigmoid")
        ret_gated = sem("ret_gated")
        ret_transposed = sem("ret_transposed")
        ret_hi = sem("ret_hi")
        ret_lo = sem("ret_lo")
        sums_taken = sem("sums_taken")
        ln_var = sem("ln_var")
        ln_std = sem("ln_std")
        ple_copied = sem("ple_copied")
        conv_transposed = sem("conv_transposed")
        conv_copied = sem("conv_copied")
        conv_begun = sem("conv_begun")
        conv_group_set = sem("conv_group_set")
        gate_conv = sem("gate_conv")
        gate_sigmoid = sem("gate_sigmoid")
        up_taken = sem("up_taken")
        gated_done = sem("gated_done")
        ple_sums = sem("ple_sums")
        ple_sigmoid = sem("ple_sigmoid")
        ple_used = sem("ple_used")
        g_hi = sem("g_hi")
        g_split = sem("g_split")
        waits_met = sem("waits_met")
        act_step = sem("act_step")
        dve_step = sem("dve_step")

        def stand_alone(eng):
            eng.sem_inc(waits_met, 1)

        block = ctx.enter_context(nc.Block())

        @block.sync
        def _(sp):
            def load(l, at, i, step, src, shape):
                s = at % RAW_SLOTS
                k, w = shape
                sp.wait_ge(panels_split, layered(l, PANELS, at + 1) + i * step)
                sp.dma_start(raw[:, s, :].rearrange("p (k w) -> p k w", k=k),
                             src.rearrange("(k p) w -> p k w", p=P)).then_inc(raw_arrived[s], 16)

            sp.dma_start(xt[:, :, :], a["x"][0].rearrange("(m p) c -> p m c", p=P)).then_inc(x_loaded, 16)
            with sp.Fori(0, DEPTH) as l:
                for n in range(KV_PANELS):
                    load(l, KV_AT + n, 0, 0, a["w_in"][l, n * 1024:(n + 1) * 1024, AK:IN_WIDTH], (8, 256))
                with sp.Fori(0, IN_LOOPS) as i:
                    for j in range(IN_BODY):
                        load(l, IN_AT + j, i, IN_BODY,
                             a["w_in"][l, (j % 4) * 512:(j % 4 + 1) * 512, bass.ds(i * 1024 + (j // 4) * 512, 512)],
                             (4, 512))
                for n in range(OUT_PANELS):
                    load(l, OUT_AT + n, 0, 0, a["w_out"][l, n * P:(n + 1) * P, :], (1, D_MODEL))
                for n in range(PLE_PANELS):
                    load(l, PLE_AT + n, 0, 0, a["w_ple_proj"][l, n * P:(n + 1) * P, :], (1, D_MODEL))
                with sp.Fori(0, FF_GROUPS) as i:
                    for j in range(UP_BODY):
                        load(l, UP_AT + j, i, UP_BODY,
                             a["w_ffn_up"][l, (j % 4) * 512:(j % 4 + 1) * 512,
                                           bass.ds(i * 512 + (j // 4) * D_FF, 512)], (4, 512))
                for n in range(GATE_PANELS):
                    load(l, GATE_AT + n, 0, 0, a["w_ple_gate"][l, n * P:(n + 1) * P, :], (1, D_MODEL))
                with sp.Fori(0, KFF // 4) as i:
                    for j in range(4):
                        load(l, DOWN_AT + j, i, 4, a["w_ffn_down"][l, bass.ds(i * 512 + j * P, P), :], (1, D_MODEL))
            sp.wait_ge(x_normed, 2 * M * DEPTH + M)
            sp.dma_start(out[0].rearrange("(m p) c -> p m c", p=P), xt[:, :, :]).then_inc(stored, 16)
            sp.wait_ge(stored, 16)

        @block.gpsimd
        def _(pool):
            for dst, src in ((ident, "c_ident"), (band, "c_band"), (causal, "c_causal")):
                pool.dma_start(dst[:, :], a[src]).then_inc(consts_loaded, 16)
            pool.dma_start(decay[:, :, :], a["c_decay"]).then_inc(consts_loaded, 16)
            for m in range(M):
                pool.dma_start(position[:, m:m + 1],
                               a["positions"][0, m * P:(m + 1) * P].rearrange("(p o) -> p o", o=1)).then_inc(freq_loaded, 16)
            pool.dma_start(freq, a["c_freq"].to_broadcast([P, FREQS])).then_inc(freq_loaded, 16)

            def everywhere(dst, row, signal):
                pool.dma_start(dst, row.to_broadcast([P, row.shape[1]])).then_inc(signal, 16)

            pool.wait_ge(tables_made, 1)
            with pool.Fori(0, DEPTH) as l:
                pool.wait_ge(x_normed, layered(l, 2 * M, M))
                stand_alone(pool)
                pool.dma_start(p_tok, a["p"][l, 0].rearrange("(m p) c -> p m c", p=P)).then_inc(p_loaded, 16)
                everywhere(sinks[:, :], a["attn_sinks"][bass.ds(l, 1), :], sinks_loaded)
                everywhere(vec[:, 0, 0:RET_WIDTH], a["ret_norm_g"][bass.ds(l, 1), :], ret_vec_loaded)
                everywhere(vec[:, 0, RET_WIDTH:], a["ret_norm_b"][bass.ds(l, 1), :], ret_vec_loaded)
                everywhere(vec[:, 1, :], a["ln1_g"][bass.ds(l, 1), :], ln_vec_loaded)
                pool.wait_ge(ret_gated, layered(l, 1, 1))
                stand_alone(pool)
                everywhere(vec[:, 0, :], a["ln1_b"][bass.ds(l, 1), :], ln_vec_loaded)
                pool.wait_ge(x_normed, layered(l, 2 * M, 2 * M))
                stand_alone(pool)
                everywhere(vec[:, 0, :], a["b_ple_gate"][bass.ds(l, 1), :], ple_vec_loaded)
                everywhere(vec[:, 1, :], a["ln2_g"][bass.ds(l, 1), :], ln_vec_loaded)
                for k in range(3):
                    pool.dma_start(conv_rows[0:2 * KFF, k, :],
                                   a["ffn_conv_w"][l, k].rearrange("(c f) -> c f", f=P)).then_inc(conv_loaded, 16)
                pool.dma_start(conv_rows[0:2 * KFF, 3, :],
                               a["ffn_conv_b"][l].rearrange("(c f) -> c f", f=P)).then_inc(conv_loaded, 16)
                pool.wait_ge(ple_sums, layered(l, 4, 4))
                stand_alone(pool)
                everywhere(vec[:, 0, :], a["ln2_b"][bass.ds(l, 1), :], ln_vec_loaded)

        @block.scalar
        def _(act):
            link = Chain(act, act_step)

            def split(l, at, i=0, step=0):
                act.wait_ge(raw_arrived[at % RAW_SLOTS],
                            (layered(l, PANELS // RAW_SLOTS, at // RAW_SLOTS + 1) + i * (step // RAW_SLOTS)) * 16)
                act.wait_ge(panels_used, layered(l, PANELS, at + 1) + i * step)
                nc.scalar.copy(w_hi[:, at % SPLIT_SLOTS, :], raw[:, at % RAW_SLOTS, :]).then_inc(hi_split, 1)

            def used(l, n):
                return layered(l, PANELS, n + SPLIT_SLOTS)

            def take_transposed(l, first):
                for b in range(XT_BANKS):
                    act.wait_ge(transposed, layered(l, T_BANKS, first + b + 1))
                    nc.scalar.copy(xT_hi[:, 2 * b:2 * b + 2, :].rearrange("p k t -> p (k t)"),
                                   ps[:, b, :]).then_inc(xT_hi_done, 1)

            def norm_root(l, first):
                for m in range(M):
                    act.wait_ge(ln_var, layered(l, 2 * M, first + m + 1))
                    nc.scalar.activation(rstd[:, m:m + 1], rstd[:, m:m + 1], ACT.Sqrt).then_inc(ln_std, 1)

            act.sem_inc(proj_copied, 1)
            act.wait_ge(angles_reduced, 2)
            nc.scalar.activation(sine[:, :, :], angle, ACT.Sin)
            nc.scalar.activation(cosine[:, :, :], fine_k, ACT.Sin).then_inc(tables_made, 1)

            with link.loop(DEPTH, 0) as l:
                take_transposed(l, 0)
                act.wait_ge(transposed, layered(l, T_BANKS, XT_BANKS + 1))
                nc.scalar.copy(pT_hi[:, :, :].rearrange("p k t -> p (k t)"), ps[:, 0, :]).then_inc(xT_hi_done, 1)
                split(l, 0)

                for n in range(KV_PANELS):
                    split(l, KV_AT + n + 1)
                act.wait_ge(panels_used, used(l, IN_AT))
                for m in range(M):
                    nc.scalar.copy(proj[:, m, AK:IN_WIDTH], ps[:, 4 + m, 0:256]).then_inc(proj_copied, 1)
                with act.Fori(0, IN_LOOPS) as i:
                    for half in range(2):
                        for j in range(4 * half, 4 * half + 4):
                            split(l, IN_AT + j + 1, i, IN_BODY)
                        act.wait_ge(panels_used, used(l, IN_AT + 4 * half + 4) + i * IN_BODY)
                        for m in range(M):
                            nc.scalar.copy(proj[:, m, bass.ds(i * 1024 + half * 512, 512)],
                                           ps[:, 2 * half + m, :]).then_inc(proj_copied, 1)

                dst = [aqT[:, 2 * n:2 * n + 2] for n in range(4)] + [akT] \
                    + [rqT[:, 2 * n:2 * n + 2] for n in range(4)] + [rkT[:, 2 * n:2 * n + 2] for n in range(4)]
                for n in range(QK_BANKS):
                    act.wait_ge(qk_transposed, layered(l, QK_BANKS, n + 1))
                    nc.scalar.copy(dst[n].rearrange("p c t -> p (c t)"), ps[:, n % 8, :]).then_inc(qk_copied, 1)

                def exponentials(n):
                    u, keys = n % 2, P * (1 + n // 4)
                    act.wait_ge(max_done, layered(l, UNITS, n + 1))
                    for h in range(4):
                        nc.scalar.activation(probs[u][:, h, 0:keys], probs[u][:, h, 0:keys], ACT.Exp,
                                             bias=neg_max[u][:, h:h + 1], accum_out=row_sum[u][:, h:h + 1])
                    nc.scalar.activation(sink_gap[u], sink_gap[u], ACT.Exp).then_inc(exp_done, 1)

                def take_probsT(n):
                    u, kc = n % 2, 1 + n // 4
                    act.wait_ge(probsT_done, layered(l, UNITS, n + 1))
                    for b in range(2):
                        nc.scalar.copy(
                            probsT[u][:, 2 * b:2 * b + 2, 0:kc * P],
                            ps[:, 4 + b, :].rearrange("p (h k) -> p h k", h=2)[:, :, 0:kc * P]).then_inc(probsT_copied, 1)

                def take_attention(n):
                    m, quad = n // 4, n % 4
                    act.wait_ge(att_done, layered(l, UNITS, n + 1))
                    nc.scalar.copy(xT_hi[:, 8 + 2 * quad:10 + 2 * quad, m * P:(m + 1) * P],
                                   ps[:, 6 + n % 2, 0:256].rearrange("p (c t) -> p c t", c=2)).then_inc(att_hi, 1)

                for n in range(UNITS + 2):
                    if n < UNITS:
                        exponentials(n)
                    if 0 <= n - 1 < UNITS:
                        take_probsT(n - 1)
                    if n >= 2:
                        take_attention(n - 2)

                for h in range(RET_HEADS):
                    act.wait_ge(ret_scores_done, layered(l, RET_HEADS, h + 1))
                    nc.scalar.copy(scoresT[h % 2][:, 256:384], ps[:, h % 2, 256:384]).then_inc(ret_cross_copied, 1)
                    act.wait_ge(ret_done, layered(l, RET_HEADS, h + 1))
                    nc.scalar.copy(ret_y[:, :, h * 256:(h + 1) * 256],
                                   ps[:, 2 + h % 2, :].rearrange("p (m c) -> p m c", m=M)).then_inc(ret_copied, 1)
                nc.scalar.activation(ret_sig, proj[:, :, RG:AQ], ACT.Sigmoid).then_inc(ret_sigmoid, 1)
                act.wait_ge(ret_var, layered(l, 1, 1))
                nc.scalar.activation(ret_rstd, ret_rstd, ACT.Sqrt).then_inc(ret_std, 1)
                for b in range(4):
                    act.wait_ge(ret_transposed, layered(l, 4, b + 1))
                    nc.scalar.copy(xT_hi[:, 2 * b:2 * b + 2, :].rearrange("p k t -> p (k t)"),
                                   ps[:, 4 + b, :]).then_inc(ret_hi, 1)

                for n in range(OUT_PANELS):
                    split(l, OUT_AT + n + 1)
                norm_root(l, 0)
                for n in range(PLE_PANELS):
                    split(l, PLE_AT + n + 1)
                act.wait_ge(panels_used, used(l, UP_AT))
                for b in range(8):
                    nc.scalar.copy(ple[:, b // 4, (b % 4) * BANK:(b % 4 + 1) * BANK], ps[:, b, :]).then_inc(ple_copied, 1)
                take_transposed(l, XT_BANKS + 1)
                act.wait_ge(conv_transposed, layered(l, 1, 1))
                nc.scalar.copy(conv, ps[:, 4, 0:4 * 2 * KFF].rearrange("p (k c) -> p k c", k=4)).then_inc(conv_copied, 1)

                stand_alone(act)
                with act.Fori(0, FF_GROUPS) as i:
                    for half in range(2):
                        for j in range(4 * half, 4 * half + 4):
                            split(l, UP_AT + j + 1, i, UP_BODY)
                        act.wait_ge(panels_used, used(l, UP_AT + 4 * half + 4) + i * UP_BODY)
                        if half == 0:
                            act.wait_ge(conv_group_set, layered(l, FF_GROUPS, 1) + i)
                        for c in range(FF_GROUP):
                            if half == 0:
                                dst = work[:, bass.ds(i * (FF_GROUP * SEQ) + c * SEQ, SEQ)]
                            else:
                                dst = tmp[1][:, c * SEQ:(c + 1) * SEQ]
                            last = nc.scalar.activation(
                                dst, ps[:, 2 * half + c // 2, (c % 2) * SEQ:(c % 2 + 1) * SEQ], ACT.Identity,
                                bias=conv_group[:, 3, half, c:c + 1], scale=conv_group[:, 2, half, c:c + 1])
                            if c % 2:
                                last.then_inc(conv_begun, 1)
                        if half == 0:
                            act.wait_ge(gate_conv, layered(l, FF_GROUPS, 2) + i)
                            stand_alone(act)
                            nc.scalar.activation(tmp[0], work[:, bass.ds(i * (FF_GROUP * SEQ), FF_GROUP * SEQ)],
                                                 ACT.Sigmoid).then_inc(gate_sigmoid, 1)

                for n in range(GATE_PANELS - 1):
                    split(l, GATE_AT + n + 1)
                for n in range(4):
                    act.wait_ge(ple_sums, layered(l, 4, n + 1))
                    nc.scalar.activation(tmp[n % 2], tmp[n % 2], ACT.Sigmoid).then_inc(ple_sigmoid, 1)

                with act.Fori(0, KFF // 4) as i:
                    for j in range(4):
                        split(l, DOWN_AT + j, i, 4)
                        act.wait_ge(panels_used, used(l, DOWN_AT + j - 3) + i * 4)
                        nc.scalar.copy(xT_hi[:, j, :], work[:, bass.ds(i * (4 * SEQ) + j * SEQ, SEQ)]).then_inc(g_hi, 1)
                norm_root(l, M)

        @block.vector
        def _(dve):
            link = Chain(dve, dve_step)
            tt, ts, stt = nc.vector.tensor_tensor, nc.vector.tensor_scalar, nc.vector.scalar_tensor_tensor

            def used(l, n):
                return layered(l, PANELS, n + SPLIT_SLOTS)

            def split(l, at, i=0, step=0):
                dve.wait_ge(hi_split, layered(l, PANELS, at + 1) + i * step)
                tt(w_lo[:, at % SPLIT_SLOTS, :], raw[:, at % RAW_SLOTS, :],
                   w_hi[:, at % SPLIT_SLOTS, :].bitcast(F32), ALU.subtract).then_inc(panels_split, 1)

            def take_transposed(l, first):
                for b in range(XT_BANKS):
                    dve.wait_ge(xT_hi_done, layered(l, T_BANKS, first + b + 1))
                    tt(xT_lo[:, 2 * b:2 * b + 2, :].rearrange("p k t -> p (k t)"), ps[:, b, :],
                       xT_hi[:, 2 * b:2 * b + 2, :].rearrange("p k t -> p (k t)").bitcast(F32),
                       ALU.subtract).then_inc(xT_lo_done, 1)

            def add_and_norm(l, products, factor, first):
                dve.wait_ge(panels_used, used(l, products))
                for m in range(M):
                    for n in range(4):
                        part = xt[:, m, n * BANK:(n + 1) * BANK]
                        stt(part, part, factor, ps[:, 4 * m + n, :], ALU.mult, ALU.add).then_inc(sums_taken, 1)
                    dve.wait_ge(sums_taken, layered(l, 16, 8 * first // M + 4 * m + 4))
                    for n in range(4):
                        last = nc.vector.bn_stats(stats[:, m, 6 * n:6 * n + 6], xt[:, m, n * BANK:(n + 1) * BANK])
                    link(last)
                    stand_alone(dve)
                    link(nc.vector.bn_aggr(moments[:, m, :], stats[:, m, :]))
                    ts(rstd[:, m:m + 1], moments[:, m, 1:2], LN_EPS, None, ALU.add).then_inc(ln_var, 1)
                dve.wait_ge(ln_vec_loaded, layered(l, 64, 32 * (1 + first // M)))
                for m in range(M):
                    dve.wait_ge(ln_std, layered(l, 2 * M, first + m + 1))
                    link(nc.vector.reciprocal(rstd[:, m:m + 1], rstd[:, m:m + 1]))
                    link(stt(xt[:, m, :], xt[:, m, :], moments[:, m, 0:1], vec[:, 1, :], ALU.subtract, ALU.mult))
                    stt(xt[:, m, :], xt[:, m, :], rstd[:, m:m + 1], vec[:, 0, :],
                        ALU.mult, ALU.add).then_inc(x_normed, 1)

            def rotate(heads, table, m):
                n, half = heads.shape[1], heads.shape[3]
                x1, x2 = heads[:, :, 0, :], heads[:, :, 1, :]
                cos = cosine[:, m, table:table + half].unsqueeze(1).to_broadcast([P, n, half])
                sin = sine[:, m, table:table + half].unsqueeze(1).to_broadcast([P, n, half])
                x1_sin = rot_a[:, 0:n * half].rearrange("p (h f) -> p h f", h=n)
                x2_sin = rot_b[:, 0:n * half].rearrange("p (h f) -> p h f", h=n)
                tt(x1_sin, x1, sin, ALU.mult)
                link(tt(x2_sin, x2, sin, ALU.mult))
                tt(x1, x1, cos, ALU.mult)
                link(tt(x2, x2, cos, ALU.mult))
                tt(x1, x1, x2_sin, ALU.subtract)
                link(tt(x2, x2, x1_sin, ALU.add))

            dve.sem_inc(panels_split, RAW_SLOTS)
            dve.sem_inc(gate_conv, 1)
            dve.sem_inc(up_taken, 1)
            dve.sem_inc(x_normed, M)

            dve.wait_ge(freq_loaded, 16 * (M + 1))
            link(nc.vector.tensor_copy(position_f[:, :], position[:, :]))
            for m in range(M):
                last = ts(angle[:, m, :], freq, position_f[:, m:m + 1], None, ALU.mult)
            link(last)

            def turns(dst, src, turn):
                link(ts(dst, src, 1.0 / turn, ROUND, ALU.mult, ALU.add))
                link(ts(dst, dst, ROUND, None, ALU.subtract))

            def less(k, part):
                link(stt(angle, k, -part, angle, ALU.mult, ALU.add))

            turns(coarse_k, angle, 2.0 * np.pi * PERIODS)
            for part in COARSE[0:3]:
                less(coarse_k, part)
            link(stt(fine_k, coarse_k, -COARSE[3], angle, ALU.mult, ALU.add))
            turns(fine_k, fine_k, 2.0 * np.pi)
            for k, part in ((fine_k, FINE[0]), (coarse_k, COARSE[3]), (fine_k, FINE[1]), (coarse_k, COARSE[4]),
                            (fine_k, FINE[2]), (coarse_k, COARSE[5]), (coarse_k, COARSE[6])):
                less(k, part)
            pi = float(np.nextafter(np.float32(np.pi), np.float32(0)))
            link(ts(angle, angle, pi, -pi, ALU.min, ALU.max))
            link(stt(fine_k, angle, -1.0, angle, ALU.mult, ALU.max))
            ts(fine_k, fine_k, -1.0, float(np.pi / 2), ALU.mult, ALU.add).then_inc(angles_reduced, 2)

            with link.loop(DEPTH, LINKS) as l:
                take_transposed(l, 0)
                dve.wait_ge(xT_hi_done, layered(l, T_BANKS, XT_BANKS + 1))
                tt(pT_lo[:, :, :].rearrange("p k t -> p (k t)"), ps[:, 0, :],
                   pT_hi[:, :, :].rearrange("p k t -> p (k t)").bitcast(F32), ALU.subtract).then_inc(xT_lo_done, 1)
                split(l, 0)
                for n in range(KV_PANELS):
                    split(l, KV_AT + n + 1)
                stand_alone(dve)
                with dve.Fori(0, IN_LOOPS) as i:
                    for j in range(IN_BODY):
                        split(l, IN_AT + j + 1, i, IN_BODY)

                dve.wait_ge(tables_made, 1)
                dve.wait_ge(consts_loaded, 64)
                dve.wait_ge(proj_copied, layered(l, COPIES, COPIES + 1))
                for m in range(M):
                    rotate(proj[:, m, AQ:AV].rearrange("p (h e f) -> p h e f", e=2, f=ATT_DIM // 2), RET_DIM // 2, m)
                    for kv in range(ATT_KV):
                        k = proj[:, m, AK + kv * ATT_DIM:AK + (kv + 1) * ATT_DIM]
                        last = nc.vector.tensor_copy(k_twice[:, m, kv, :, :],
                                                     k.unsqueeze(1).to_broadcast([P, 2, ATT_DIM]))
                    link(last)
                for m in range(M):
                    rotate(proj[:, m, RQ:RV].rearrange("p (h e f) -> p h e f", e=2, f=RET_DIM // 2), 0, m)
                    heads = proj[:, m, RQ:RV].rearrange("p (h c) -> p h c", c=RET_DIM)
                    link(tt(heads, heads, decay[:, m, :].unsqueeze(2).to_broadcast([P, 2 * RET_HEADS, RET_DIM]),
                            ALU.mult))
                dve.sem_inc(rotated, 1)

                dve.wait_ge(sinks_loaded, layered(l, 16, 16))

                def maxima(n):
                    u, quad, keys = n % 2, n % 4, P * (1 + n // 4)
                    mask = (band[:, P:] if n < 4 else band[:, :]).unsqueeze(1).to_broadcast([P, 2, keys])
                    dve.wait_ge(scores_done, layered(l, UNITS, n + 1))
                    if n >= 2:
                        dve.wait_ge(probsT_done, layered(l, UNITS, n - 1))
                    for e in range(2):
                        scores = ps[:, 2 * u + e, :].rearrange("p (c k) -> p c k", c=2)[:, :, 0:keys]
                        last = stt(probs[u].rearrange("p (c e) k -> p e c k", e=2)[:, e, :, 0:keys], scores,
                                   ATT_DIM ** -0.5, mask, ALU.mult, ALU.add)
                    link(last)
                    sink = sinks[:, 4 * quad:4 * quad + 4]
                    link(nc.vector.reduce_max(row_max[u], probs[u][:, :, 0:keys], AX_X))
                    link(tt(row_max[u], row_max[u], sink, ALU.max))
                    ts(neg_max[u], row_max[u], -1.0, None, ALU.mult)
                    tt(sink_gap[u], sink, row_max[u], ALU.subtract).then_inc(max_done, 1)

                def normalise(n):
                    u, keys = n % 2, P * (1 + n // 4)
                    dve.wait_ge(exp_done, layered(l, UNITS, n + 1))
                    link(tt(row_sum[u], row_sum[u], sink_gap[u], ALU.add))
                    link(nc.vector.reciprocal(row_sum[u], row_sum[u]))
                    p = probs[u][:, :, 0:keys]
                    tt(p, p, row_sum[u].unsqueeze(2).to_broadcast([P, 4, keys]), ALU.mult).then_inc(probs_done, 1)

                def take_attention(n):
                    m, quad = n // 4, n % 4
                    dve.wait_ge(att_hi, layered(l, UNITS, n + 1))
                    part = (slice(None), slice(8 + 2 * quad, 10 + 2 * quad), slice(m * P, (m + 1) * P))
                    tt(xT_lo[part], ps[:, 6 + n % 2, 0:256].rearrange("p (c t) -> p c t", c=2),
                       xT_hi[part].bitcast(F32), ALU.subtract).then_inc(att_lo, 1)

                maxima(0)
                for n in range(UNITS):
                    if n + 1 < UNITS:
                        maxima(n + 1)
                    normalise(n)
                    if n >= 2:
                        take_attention(n - 2)
                for n in (UNITS - 2, UNITS - 1):
                    take_attention(n)

                for h in range(RET_HEADS):
                    dve.wait_ge(ret_cross_copied, layered(l, RET_HEADS, h + 1))
                    tt(scoresT[h % 2][:, 0:256].rearrange("p (b t) -> p b t", b=2),
                       ps[:, h % 2, 0:256].rearrange("p (b t) -> p b t", b=2),
                       causal[:, :].unsqueeze(1).to_broadcast([P, 2, P]), ALU.mult).then_inc(ret_scores_masked, 1)
                for h in range(RET_HEADS):
                    dve.wait_ge(ret_copied, layered(l, RET_HEADS, h + 1))
                    for m in range(M):
                        link(nc.vector.bn_stats(ret_stats, ret_y[:, m, h * RET_DIM:(h + 1) * RET_DIM]))
                        stand_alone(dve)
                        link(nc.vector.bn_aggr(ret_moments[:, m, h, :], ret_stats))
                ts(ret_rstd, ret_moments[:, :, :, 1], GN_EPS, None, ALU.add).then_inc(ret_var, 1)
                dve.wait_ge(ret_sigmoid, layered(l, 1, 1))
                link(tt(ret_sig, ret_sig, proj[:, :, RG:AQ], ALU.mult))
                dve.wait_ge(ret_std, layered(l, 1, 1))
                link(nc.vector.reciprocal(ret_rstd, ret_rstd))
                for m in range(M):
                    for h in range(RET_HEADS):
                        y = ret_y[:, m, h * RET_DIM:(h + 1) * RET_DIM]
                        last = ts(y, y, ret_moments[:, m, h, 0:1], ret_rstd[:, m, h:h + 1], ALU.subtract, ALU.mult)
                link(last)
                dve.wait_ge(ret_vec_loaded, layered(l, 32, 32))
                for v, op in ((vec[:, 0, 0:RET_WIDTH], ALU.mult), (vec[:, 0, RET_WIDTH:], ALU.add)):
                    link(tt(ret_y, ret_y, v.unsqueeze(1).to_broadcast([P, M, RET_WIDTH]), op))
                tt(ret_y, ret_y, ret_sig, ALU.mult).then_inc(ret_gated, 1)
                for b in range(4):
                    dve.wait_ge(ret_hi, layered(l, 4, b + 1))
                    tt(xT_lo[:, 2 * b:2 * b + 2, :].rearrange("p k t -> p (k t)"), ps[:, 4 + b, :],
                       xT_hi[:, 2 * b:2 * b + 2, :].rearrange("p k t -> p (k t)").bitcast(F32),
                       ALU.subtract).then_inc(ret_lo, 1)

                for n in range(OUT_PANELS):
                    split(l, OUT_AT + n + 1)
                add_and_norm(l, PLE_AT, ALPHA, 0)
                for n in range(PLE_PANELS):
                    split(l, PLE_AT + n + 1)
                take_transposed(l, XT_BANKS + 1)
                dve.wait_ge(conv_copied, layered(l, 1, 1))

                stand_alone(dve)
                with link.loop(FF_GROUPS, UP_LINKS) as i:
                    for half in range(2):
                        link(nc.vector.tensor_copy(conv_group[:, :, half, :],
                                                   conv[:, :, bass.ds(i * FF_GROUP + half * KFF, FF_GROUP)]))
                    dve.sem_inc(conv_group_set, 1)
                    for half in range(2):
                        for j in range(4 * half, 4 * half + 4):
                            split(l, UP_AT + j + 1, i, UP_BODY)
                        for b in range(2):
                            dve.wait_ge(conv_begun, layered(l, 4 * FF_GROUPS, 2 * half + b + 1) + i * 4)
                            for back in (1, 2):
                                for c in (2 * b, 2 * b + 1):
                                    u = ps[:, 2 * half + b, (c % 2) * SEQ:(c % 2 + 1) * SEQ - back]
                                    if half == 0:
                                        dst = work[:, bass.ds(i * (FF_GROUP * SEQ) + c * SEQ + back, SEQ - back)]
                                    else:
                                        dst = tmp[1][:, c * SEQ + back:(c + 1) * SEQ]
                                    last = stt(dst, u, conv_group[:, 2 - back, half, c:c + 1], dst, ALU.mult, ALU.add)
                                link(last)
                        group = work[:, bass.ds(i * (FF_GROUP * SEQ), FF_GROUP * SEQ)]
                        if half == 0:
                            dve.sem_inc(gate_conv, 1)
                            dve.wait_ge(gate_sigmoid, layered(l, FF_GROUPS, 1) + i)
                            link(tt(group, group, tmp[0], ALU.mult))
                        else:
                            dve.sem_inc(up_taken, 1)
                            link(tt(group, group, tmp[1], ALU.mult))
                dve.sem_inc(gated_done, 1)

                for n in range(GATE_PANELS - 1):
                    split(l, GATE_AT + n + 1)
                dve.wait_ge(ple_vec_loaded, layered(l, 16, 16))
                dve.wait_ge(panels_used, used(l, DOWN_AT))
                for n in range(4):
                    m, cols = n // 2, slice((n % 2) * 1024, (n % 2 + 1) * 1024)
                    tt(tmp[n % 2].rearrange("p (b c) -> p b c", b=2), ps[:, 2 * n:2 * n + 2, :],
                       vec[:, 0, cols].rearrange("p (b c) -> p b c", b=2), ALU.add).then_inc(ple_sums, 1)
                    if n % 2:
                        for k in (n - 1, n):
                            c = slice((k % 2) * 1024, (k % 2 + 1) * 1024)
                            dve.wait_ge(ple_sigmoid, layered(l, 4, k + 1))
                            link(tt(ple[:, m, c], ple[:, m, c], tmp[k % 2], ALU.mult))
                            link(stt(xt[:, m, c], xt[:, m, c], ALPHA, ple[:, m, c], ALU.mult, ALU.add))

                stand_alone(dve)
                with dve.Fori(0, KFF // 4) as i:
                    for j in range(4):
                        split(l, DOWN_AT + j, i, 4)
                        dve.wait_ge(g_hi, layered(l, KFF, j + 1) + i * 4)
                        tt(xT_lo[:, j, :], work[:, bass.ds(i * (4 * SEQ) + j * SEQ, SEQ)],
                           xT_hi[:, j, :].bitcast(F32), ALU.subtract).then_inc(g_split, 1)
                add_and_norm(l, PANELS, 1.0, M)

        @block.tensor
        def _(pe):
            mm = nc.tensor.matmul

            def panel(l, at, i, step, products):
                pe.wait_ge(panels_split, layered(l, PANELS, at + 1 + RAW_SLOTS) + i * step)
                for bank, hi, lo, x_hi, x_lo, first, last, flip in products:
                    pairs = ((x_hi, lo), (x_hi, hi), (x_lo, hi))
                    for n, (x, w) in enumerate(pairs):
                        lhs, rhs = (w, x) if flip else (x, w)
                        done = mm(bank, lhs, rhs, start=first and n == 0, stop=last and n == 2,
                                  skip_group_check=flip)
                done.then_inc(panels_used, 1)

            def tokens_by_columns(s, k_chunks, width, x_slots, banks, first, last, xh=xT_hi, xl=xT_lo):
                found = []
                for k in range(k_chunks):
                    for m in range(M):
                        for n in range((width + BANK - 1) // BANK):
                            lo, hi = k * width + n * BANK, k * width + min(width, (n + 1) * BANK)
                            x = (slice(None), x_slots[k], slice(m * P, (m + 1) * P))
                            found.append((banks(m, n)[:, 0:hi - lo], w_hi[:, s, lo:hi], w_lo[:, s, lo:hi], xh[x], xl[x],
                                          first and k == 0, last and k == k_chunks - 1, False))
                return found

            def transpose(dst, src):
                return nc.tensor.transpose(dst, src, ident[:, :])

            def transpose_x(l, first):
                for b in range(XT_BANKS):
                    for k in (2 * b, 2 * b + 1):
                        for m in range(M):
                            col = (k % 2) * SEQ + m * P
                            last = transpose(ps[:, b, col:col + P], xt[:, m, k * P:(k + 1) * P])
                    last.then_inc(transposed, 1)

            def wide(l, at, n, k, banks8=lambda m, n: ps[:, 4 * m + n, :], last=False, i=0, step=0, first=False,
                     slot=None, xh=xT_hi, xl=xT_lo):
                panel(l, at + n, i, step,
                      tokens_by_columns((at + n) % SPLIT_SLOTS, 1, D_MODEL, [k if slot is None else slot], banks8,
                                        first, last, xh, xl))

            pe.sem_inc(panels_used, SPLIT_SLOTS)
            pe.wait_ge(x_loaded, 16)
            pe.wait_ge(consts_loaded, 64)

            with pe.Fori(0, DEPTH) as l:
                pe.wait_ge(x_normed, layered(l, 2 * M, M))
                transpose_x(l, 0)
                pe.wait_ge(p_loaded, layered(l, 16, 16))
                pe.wait_ge(xT_lo_done, layered(l, T_BANKS, 1))
                for k in range(PLE_PANELS):
                    for m in range(M):
                        last = transpose(ps[:, 0, k * SEQ + m * P:k * SEQ + (m + 1) * P], p_tok[:, m, k * P:(k + 1) * P])
                last.then_inc(transposed, 1)

                pe.wait_ge(xT_lo_done, layered(l, T_BANKS, XT_BANKS + 1))
                for n in range(KV_PANELS):
                    panel(l, KV_AT + n, 0, 0,
                          tokens_by_columns((KV_AT + n) % SPLIT_SLOTS, 8, 256, range(8 * n, 8 * n + 8),
                                            lambda m, n: ps[:, 4 + m, :], n == 0, n == 1))
                with pe.Fori(0, IN_LOOPS) as i:
                    for half in range(2):
                        pe.wait_ge(proj_copied, layered(l, COPIES, 2 * half + 1) + i * 4)
                        for j in range(4):
                            at = IN_AT + 4 * half + j
                            panel(l, at, i, IN_BODY,
                                  tokens_by_columns(at % SPLIT_SLOTS, 4, 512, range(4 * j, 4 * j + 4),
                                                    lambda m, n: ps[:, 2 * half + m, :], j == 0, j == 3))

                pe.wait_ge(rotated, layered(l, 1, 1))
                pe.wait_ge(proj_copied, layered(l, COPIES, COPIES + 1))
                sources = [[[proj[:, m, AQ + c * P:AQ + (c + 1) * P] for m in range(M)] for c in range(8)],
                           [[k_twice[:, m, kv, :, :].rearrange("p e d -> p (e d)") for m in range(M)]
                            for kv in range(ATT_KV)],
                           [[proj[:, m, c * P:(c + 1) * P] for m in range(M)] for c in range(16)]]
                chunks = [c for s in sources for c in s]
                for n in range(QK_BANKS):
                    if n == 0:
                        pass
                    if n >= 8:
                        pe.wait_ge(qk_copied, layered(l, QK_BANKS, n - 7))
                    for c in (0, 1):
                        for m in range(M):
                            last = transpose(ps[:, n % 8, c * SEQ + m * P:c * SEQ + (m + 1) * P], chunks[2 * n + c][m])
                    last.then_inc(qk_transposed, 1)
                pe.wait_ge(qk_copied, layered(l, QK_BANKS, QK_BANKS))

                def scores(n):
                    m, quad, u, keys = n // 4, n % 4, n % 2, P * (1 + n // 4)
                    if n >= 2:
                        pe.wait_ge(max_done, layered(l, UNITS, n - 1))
                    for c in range(2):
                        for e in range(2):
                            half = slice(64 * e, 64 * e + 64)
                            last = mm(ps[:, 2 * u + e, c * 256:c * 256 + keys],
                                      aqT[half, 2 * quad + c, m * P:(m + 1) * P],
                                      akT[half, quad // 2, 0:keys], start=True, stop=True)
                    last.then_inc(scores_done, 1)

                def transpose_probs(n):
                    u, kc = n % 2, 1 + n // 4
                    pe.wait_ge(probs_done, layered(l, UNITS, n + 1))
                    if n >= 1:
                        pe.wait_ge(probsT_copied, layered(l, 2 * UNITS, 2 * n))
                    for h in range(4):
                        for k in range(kc):
                            col = (h % 2) * 256 + k * P
                            last = transpose(ps[:, 4 + h // 2, col:col + P], probs[u][:, h, k * P:(k + 1) * P])
                    last.then_inc(probsT_done, 1)

                def attend(n):
                    quad, u, kc = n % 4, n % 2, 1 + n // 4
                    pe.wait_ge(probsT_copied, layered(l, 2 * UNITS, 2 * n + 2))
                    if n >= 2:
                        pe.wait_ge(att_lo, layered(l, UNITS, n - 1))
                    v = slice(AV + (quad // 2) * ATT_DIM, AV + (quad // 2 + 1) * ATT_DIM)
                    for c in range(2):
                        for e in range(2):
                            for k in range(kc):
                                last = mm(ps[64 * e:64 * e + 64, 6 + n % 2, c * P:(c + 1) * P], proj[:, k, v],
                                          probsT[u][:, 2 * c + e, k * P:(k + 1) * P], start=k == 0, stop=k == kc - 1)
                    last.then_inc(att_done, 1)

                scores(0)
                scores(1)
                for n in range(UNITS):
                    transpose_probs(n)
                    if n + 2 < UNITS:
                        scores(n + 2)
                    attend(n)

                pe.wait_ge(att_lo, layered(l, UNITS, UNITS))

                def ret_scores(h):
                    if h >= 2:
                        pe.wait_ge(ret_scores_masked, layered(l, RET_HEADS, h - 1))
                    for col, j, i in ((0, 0, 0), (P, 1, 1), (2 * P, 0, 1)):
                        for k in range(2):
                            last = mm(ps[:, h % 2, col:col + P], rkT[:, 2 * h + k, j * P:(j + 1) * P],
                                      rqT[:, 2 * h + k, i * P:(i + 1) * P], start=k == 0, stop=k == 1)
                    last.then_inc(ret_scores_done, 1)

                ret_scores(0)
                ret_scores(1)
                for h in range(RET_HEADS):
                    pe.wait_ge(ret_scores_masked, layered(l, RET_HEADS, h + 1))
                    if h >= 2:
                        pe.wait_ge(ret_copied, layered(l, RET_HEADS, h - 1))
                    s, cols = scoresT[h % 2], slice(RV + h * RET_DIM, RV + (h + 1) * RET_DIM)
                    y = ps[:, 2 + h % 2, :].rearrange("p (m c) -> p m c", m=M)
                    mm(y[:, 0, :], s[:, 0:P], proj[:, 0, cols], start=True, stop=True)
                    mm(y[:, 1, :], s[:, 2 * P:3 * P], proj[:, 0, cols], start=True, stop=False)
                    mm(y[:, 1, :], s[:, P:2 * P], proj[:, 1, cols], start=False, stop=True).then_inc(ret_done, 1)
                    if h + 2 < RET_HEADS:
                        ret_scores(h + 2)
                pe.wait_ge(ret_gated, layered(l, 1, 1))
                for b in range(4):
                    for c in (0, 1):
                        for m in range(M):
                            last = transpose(ps[:, 4 + b, c * SEQ + m * P:c * SEQ + (m + 1) * P],
                                             ret_y[:, m, (2 * b + c) * P:(2 * b + c + 1) * P])
                    last.then_inc(ret_transposed, 1)

                pe.wait_ge(ret_lo, layered(l, 4, 4))
                for n in range(OUT_PANELS):
                    wide(l, OUT_AT, n, n, first=n == 0, last=n == OUT_PANELS - 1)

                pe.wait_ge(sums_taken, layered(l, 16, 8))
                for n in range(PLE_PANELS):
                    wide(l, PLE_AT, n, n, first=n == 0, last=n == PLE_PANELS - 1, xh=pT_hi, xl=pT_lo)

                pe.wait_ge(x_normed, layered(l, 2 * M, 2 * M))
                pe.wait_ge(ple_copied, layered(l, 8, 8))
                transpose_x(l, XT_BANKS + 1)
                pe.wait_ge(conv_loaded, layered(l, 64, 64))
                pe.wait_ge(xT_lo_done, layered(l, T_BANKS, T_BANKS - 3))
                for k in range(4):
                    last = nc.tensor.transpose(ps[:, 4, k * 2 * KFF:(k + 1) * 2 * KFF], conv_rows[0:2 * KFF, k, :],
                                               ident[0:2 * KFF, 0:2 * KFF])
                last.then_inc(conv_transposed, 1)

                pe.wait_ge(xT_lo_done, layered(l, T_BANKS, T_BANKS))
                stand_alone(pe)
                with pe.Fori(0, FF_GROUPS) as i:
                    for half in range(2):
                        if half == 0:
                            pe.wait_ge(gate_conv, layered(l, FF_GROUPS, 1) + i)
                        else:
                            pe.wait_ge(up_taken, layered(l, FF_GROUPS, 1) + i)
                        for j in range(4):
                            at = UP_AT + 4 * half + j
                            s = at % SPLIT_SLOTS
                            products = []
                            for k in range(4):
                                for c in range(FF_GROUP):
                                    w = slice(k * 512 + c * P, k * 512 + (c + 1) * P)
                                    products.append((ps[:, 2 * half + c // 2, (c % 2) * SEQ:(c % 2 + 1) * SEQ],
                                                     w_hi[:, s, w], w_lo[:, s, w],
                                                     xT_hi[:, 4 * j + k, :], xT_lo[:, 4 * j + k, :],
                                                     j == 0 and k == 0 and c % 2 == 0, j == 3 and k == 3, True))
                            panel(l, at, i, UP_BODY, products)

                pe.wait_ge(gate_conv, layered(l, FF_GROUPS, FF_GROUPS + 1))
                pe.wait_ge(up_taken, layered(l, FF_GROUPS, FF_GROUPS + 1))
                for n in range(GATE_PANELS):
                    wide(l, GATE_AT, n, n, first=n == 0, last=n == GATE_PANELS - 1)

                pe.wait_ge(ple_sums, layered(l, 4, 4))

                def down(j, i, first, last):
                    pe.wait_ge(g_split, layered(l, KFF, j % 4 + 1) + i * 4)
                    wide(l, DOWN_AT, j % 4, j % 4, i=i, step=4, first=first, last=last)

                for j in range(4):
                    down(j, 0, j == 0, False)
                with pe.Fori(1, KFF // 4 - 1) as i:
                    for j in range(4):
                        down(j, i, False, False)
                for j in range(4):
                    down(j, KFF // 4 - 1, False, j == 3)


UP_LINKS = 2 + 2 * 4 + 2
LINKS = (3 + 1) * 2 + (3 + 1) * 2 + UNITS * 3 + UNITS * 2 + 2 * RET_HEADS * M + 5 + 2 * (2 * M + 2 * M) + FF_GROUPS * UP_LINKS + 8


def constants():
    f = np.float32
    ret = f(1.0) / np.power(f(10000.0), np.linspace(0.0, 1.0, RET_DIM // 2, dtype=f))
    att = np.power(f(10000.0), -np.arange(0, ATT_DIM, 2, dtype=f) / f(ATT_DIM))
    i = np.arange(P)
    later = i[:, None] >= i[None, :]
    band = np.where(np.concatenate([~later, later], 1), 0.0, MASKED)
    gamma = np.log1p(-np.exp2(-5.0 - np.arange(RET_HEADS)))
    t = (np.arange(SEQ) - SEQ // 2)[:, None]
    decay = np.concatenate([np.exp(gamma * t), np.exp(-gamma * t) * RET_DIM ** -0.5], 1)
    return {
        "c_freq": np.concatenate([ret, att])[None, :].astype(f),
        "c_ident": np.eye(P, dtype=f),
        "c_band": band.astype(f),
        "c_causal": (i[:, None] <= i[None, :]).astype(f),
        "c_decay": np.ascontiguousarray(decay.reshape(M, P, 2 * RET_HEADS).transpose(1, 0, 2)).astype(f),
    }


def kernel(**inputs):
    import concourse.bacc as bacc
    from concourse.bass_utils import run_bass_kernel_spmd

    nc = bacc.Bacc("TRN2", target_bir_lowering=False, num_devices=1)
    arrays, aps = {}, {}
    for name, value in [*inputs.items(), *constants().items()]:
        value = np.ascontiguousarray(value)
        arrays[f"in_{name}"] = value
        aps[name] = nc.dram_tensor(f"in_{name}", value.shape, mybir.dt.from_np(value.dtype), kind="ExternalInput").ap()
    out = nc.dram_tensor("out_x", (1, SEQ, D_MODEL), F32, kind="ExternalOutput").ap()
    build(nc, aps, out)
    result = run_bass_kernel_spmd(nc, [arrays], core_ids=[0])
    return result.results[0]["out_x"]
```

```python
from contextlib import ExitStack, contextmanager

import numpy as np
import concourse.bass as bass
from concourse import mybir

F32 = mybir.dt.float32
F32R = mybir.dt.float32r
I32 = mybir.dt.int32
ALU = mybir.AluOpType
ACT = mybir.ActivationFunctionType
AX_X = mybir.AxisListType.X

P = 128
D_MODEL, SEQ, DEPTH, PLE_DIM = 2048, 256, 2, 256
D_FF = 5632
M = SEQ // P
KD = D_MODEL // P
RET_HEADS, RET_DIM = 4, 256
RET_WIDTH = RET_HEADS * RET_DIM
ATT_HEADS, ATT_KV, ATT_DIM = 16, 2, 64
ATT_WIDTH = ATT_HEADS * ATT_DIM
RQ, RK, RV, RG, AQ = (n * RET_WIDTH for n in range(5))
AK = AQ + ATT_WIDTH
AV = AK + ATT_KV * ATT_DIM
IN_WIDTH = AV + ATT_KV * ATT_DIM
FREQS = RET_DIM // 2 + ATT_DIM // 2
ALPHA = float((2 * DEPTH) ** 0.25)
LN_EPS, GN_EPS = 1e-5, 1e-6
MASKED = -3.0e38

PANEL = 2048
RAW_SLOTS, SPLIT_SLOTS = 4, 2
BANK = 512
FF_GROUP = 4
FF_GROUPS = D_FF // P // FF_GROUP
KFF = D_FF // P

KV_PANELS = 2
IN_LOOPS, IN_BODY = AK // 1024, 8
OUT_PANELS = KD
PLE_PANELS = PLE_DIM // P
UP_BODY = 8
GATE_PANELS = KD
KV_AT = 0
IN_AT = KV_AT + KV_PANELS
OUT_AT = IN_AT + IN_LOOPS * IN_BODY
PLE_AT = OUT_AT + OUT_PANELS
GATE_AT = PLE_AT + PLE_PANELS
UP_AT = GATE_AT + GATE_PANELS
DOWN_AT = UP_AT + FF_GROUPS * UP_BODY
PANELS = DOWN_AT + KFF

COPIES = 2 * (1 + 2 * IN_LOOPS)
XT_BANKS = KD // 2
T_BANKS = 2 * XT_BANKS + 1
QK_BANKS = 4 + 1 + 4 + 4
UNITS = M * ATT_KV * 2
TAPS = 2 * FF_GROUPS
NORMS = 4


def layered(l, per_layer, n):
    return l * per_layer + n


class Chain:

    def __init__(self, eng, sem):
        self.eng, self.sem, self.base, self.n = eng, sem, 0, 0

    def __call__(self, instruction):
        instruction.then_inc(self.sem, 1)
        self.n += 1
        self.eng.wait_ge(self.sem, self.base + self.n)

    @contextmanager
    def loop(self, count, links):
        base, first = self.base, self.n
        with self.eng.Fori(0, count) as i:
            self.base = base + i * links
            yield i
            assert self.n - first == links, (self.n - first, links)
        self.base, self.n = base, first + count * links


PLE_BANKS = (1, 2, 3, 4, 5, 6, 7, 0)
SCALE = 160
TWO_PI = 6283185307179586476925286766559005768394338798750 * 2 ** SCALE // 10 ** 48
PERIODS = 4096


def angle_parts(value, lowest_bits):
    parts = []
    for bit in lowest_bits:
        unit = 2 ** (SCALE + bit)
        n = (2 * value + unit) // (2 * unit)
        parts.append(float(n) * 2.0 ** bit)
        value -= n * unit
    return parts


COARSE = angle_parts(TWO_PI * PERIODS, (8, 1, -6, -13, -20, -27, -34))
FINE = angle_parts(TWO_PI, (-9, -21, -33))
ROUND = 1.5 * 2.0 ** 23


def build(nc, a, out):
    with ExitStack() as ctx:
        def sb(name, shape, dt=F32):
            return ctx.enter_context(nc.sbuf_tensor(name, shape, dt))

        def sem(name):
            return ctx.enter_context(nc.semaphore(name))

        xt = sb("xt", [P, M, D_MODEL])
        work = sb("work", [P, KFF * SEQ])
        xT_hi = sb("xT_hi", [P, KD, SEQ], F32R)
        xT_lo = sb("xT_lo", [P, KD, SEQ], F32R)
        pT_hi = sb("pT_hi", [P, PLE_PANELS, SEQ], F32R)
        pT_lo = sb("pT_lo", [P, PLE_PANELS, SEQ], F32R)
        raw = sb("raw", [P, RAW_SLOTS, PANEL])
        w_hi = sb("w_hi", [P, SPLIT_SLOTS, PANEL], F32R)
        w_lo = sb("w_lo", [P, SPLIT_SLOTS, PANEL], F32R)
        vec = sb("vec", [P, 2, D_MODEL])
        scratch = sb("scratch", [P, 6656])
        cosine = sb("cosine", [P, M, FREQS])
        sine = sb("sine", [P, M, FREQS])
        ident = sb("ident", [P, P])
        band = sb("band", [P, 2 * P])
        causal = sb("causal", [P, P])
        decay = sb("decay", [P, M, 2 * RET_HEADS])
        position = sb("position", [P, M], I32)
        position_f = sb("position_f", [P, M])
        sinks = sb("sinks", [P, ATT_HEADS])
        small = sb("small", [P, 96])

        proj = work[:, 0:M * IN_WIDTH].rearrange("p (m c) -> p m c", m=M)
        gated = work[:, :].rearrange("p (f t) -> p f t", t=SEQ)

        freq = scratch[:, 0:FREQS]
        angle = scratch[:, 320:640].rearrange("p (m f) -> p m f", m=M)
        coarse_k = scratch[:, 640:960].rearrange("p (m f) -> p m f", m=M)
        fine_k = scratch[:, 960:1280].rearrange("p (m f) -> p m f", m=M)
        p_tok = scratch[:, 0:M * PLE_DIM].rearrange("p (m c) -> p m c", m=M)
        rot_a = scratch[:, 2048:3072]
        rot_b = scratch[:, 3072:4096]
        k_twice = scratch[:, 4096:4608].rearrange("p (m k e d) -> p m k e d", m=M, k=ATT_KV, e=2)
        aqT = scratch[:, 0:2048].rearrange("p (c t) -> p c t", t=SEQ)
        akT = scratch[:, 6144:6656].rearrange("p (c t) -> p c t", t=SEQ)
        rqT = scratch[:, 2048:4096].rearrange("p (c t) -> p c t", t=SEQ)
        rkT = scratch[:, 4096:6144].rearrange("p (c t) -> p c t", t=SEQ)
        probs = [proj[:, 0, 1024 * u:1024 * (u + 1)].rearrange("p (h k) -> p h k", h=4) for u in range(2)]
        probsT = [proj[:, 1, 1024 * u:1024 * (u + 1)].rearrange("p (h k) -> p h k", h=4) for u in range(2)]
        scoresT = [proj[:, 0, 512 * u:512 * u + 384] for u in range(2)]
        ret_y = scratch[:, 0:2048].rearrange("p (m c) -> p m c", m=M)
        ret_sig = scratch[:, 2048:4096].rearrange("p (m c) -> p m c", m=M)
        ple = scratch[:, 0:4096].rearrange("p (m c) -> p m c", m=M)
        tmp = [scratch[:, 4096:5120], scratch[:, 5120:6144]]
        conv_rows = scratch[:, 4096:4608].rearrange("p (k c) -> p k c", k=4)
        conv = scratch[:, 6144:6144 + 4 * 2 * KFF].rearrange("p (k c) -> p k c", k=4)
        stats = small[:, 0:48].rearrange("p (m s) -> p m s", m=M)
        moments = small[:, 48:52].rearrange("p (m s) -> p m s", m=M)
        rstd = small[:, 52:54]
        ret_moments = small[:, 0:16].rearrange("p (m h s) -> p m h s", m=M, h=RET_HEADS)
        ret_stats = small[:, 16:22]
        ret_rstd = small[:, 24:32].rearrange("p (m h) -> p m h", m=M)
        row_max = [small[:, 54 + 4 * u:58 + 4 * u] for u in range(2)]
        neg_max = [small[:, 62 + 4 * u:66 + 4 * u] for u in range(2)]
        sink_gap = [small[:, 70 + 4 * u:74 + 4 * u] for u in range(2)]
        row_sum = [small[:, 78 + 4 * u:82 + 4 * u] for u in range(2)]
        conv_group = small[:, 0:32].rearrange("p (k h c) -> p k h c", k=4, h=2)

        ps = ctx.enter_context(nc.psum_tensor("ps", [P, 8, BANK], F32))

        raw_arrived = [sem(f"raw_arrived{s}") for s in range(RAW_SLOTS)]
        hi_split = sem("hi_split")
        panels_split = sem("panels_split")
        panels_used = sem("panels_used")
        x_loaded = sem("x_loaded")
        consts_loaded = sem("consts_loaded")
        freq_loaded = sem("freq_loaded")
        p_loaded = sem("p_loaded")
        sinks_loaded = sem("sinks_loaded")
        ret_vec_loaded = sem("ret_vec_loaded")
        ln_vec_loaded = sem("ln_vec_loaded")
        ple_vec_loaded = sem("ple_vec_loaded")
        conv_loaded = sem("conv_loaded")
        stored = sem("stored")
        angles_reduced = sem("angles_reduced")
        tables_made = sem("tables_made")
        x_normed = sem("x_normed")
        transposed = sem("transposed")
        xT_hi_done = sem("xT_hi_done")
        xT_lo_done = sem("xT_lo_done")
        proj_copied = sem("proj_copied")
        rotated = sem("rotated")
        qk_transposed = sem("qk_transposed")
        qk_copied = sem("qk_copied")
        scores_done = sem("scores_done")
        max_done = sem("max_done")
        exp_done = sem("exp_done")
        probs_done = sem("probs_done")
        probsT_done = sem("probsT_done")
        probsT_copied = sem("probsT_copied")
        att_done = sem("att_done")
        att_hi = sem("att_hi")
        att_lo = sem("att_lo")
        ret_scores_done = sem("ret_scores_done")
        ret_cross_copied = sem("ret_cross_copied")
        ret_scores_masked = sem("ret_scores_masked")
        ret_done = sem("ret_done")
        ret_copied = sem("ret_copied")
        ret_var = sem("ret_var")
        ret_std = sem("ret_std")
        ret_sigmoid = sem("ret_sigmoid")
        ret_gated = sem("ret_gated")
        ret_transposed = sem("ret_transposed")
        ret_hi = sem("ret_hi")
        ret_lo = sem("ret_lo")
        sums_taken = sem("sums_taken")
        ln_var = sem("ln_var")
        ln_std = sem("ln_std")
        ple_copied = sem("ple_copied")
        conv_transposed = sem("conv_transposed")
        conv_copied = sem("conv_copied")
        conv_begun = sem("conv_begun")
        conv_group_set = sem("conv_group_set")
        gate_conv = sem("gate_conv")
        gate_sigmoid = sem("gate_sigmoid")
        up_taken = sem("up_taken")
        ple_sums = sem("ple_sums")
        ple_sigmoid = sem("ple_sigmoid")
        ple_used = sem("ple_used")
        g_hi = sem("g_hi")
        g_split = sem("g_split")
        waits_met = sem("waits_met")
        act_step = sem("act_step")
        dve_step = sem("dve_step")

        def stand_alone(eng):
            eng.sem_inc(waits_met, 1)

        block = ctx.enter_context(nc.Block())

        @block.sync
        def _(sp):
            def load(l, at, i, step, src, shape):
                s = at % RAW_SLOTS
                k, w = shape
                sp.wait_ge(panels_split, layered(l, PANELS, at + 1) + i * step)
                sp.dma_start(raw[:, s, :].rearrange("p (k w) -> p k w", k=k),
                             src.rearrange("(k p) w -> p k w", p=P)).then_inc(raw_arrived[s], 16)

            sp.dma_start(xt[:, :, :], a["x"][0].rearrange("(m p) c -> p m c", p=P)).then_inc(x_loaded, 16)
            with sp.Fori(0, DEPTH) as l:
                for n in range(KV_PANELS):
                    load(l, KV_AT + n, 0, 0, a["w_in"][l, n * 1024:(n + 1) * 1024, AK:IN_WIDTH], (8, 256))
                with sp.Fori(0, IN_LOOPS) as i:
                    for j in range(IN_BODY):
                        load(l, IN_AT + j, i, IN_BODY,
                             a["w_in"][l, (j % 4) * 512:(j % 4 + 1) * 512, bass.ds(i * 1024 + (j // 4) * 512, 512)],
                             (4, 512))
                for n in range(OUT_PANELS):
                    load(l, OUT_AT + n, 0, 0, a["w_out"][l, n * P:(n + 1) * P, :], (1, D_MODEL))
                for n in range(PLE_PANELS):
                    load(l, PLE_AT + n, 0, 0, a["w_ple_proj"][l, n * P:(n + 1) * P, :], (1, D_MODEL))
                for n in range(GATE_PANELS):
                    load(l, GATE_AT + n, 0, 0, a["w_ple_gate"][l, n * P:(n + 1) * P, :], (1, D_MODEL))
                with sp.Fori(0, FF_GROUPS) as i:
                    for j in range(UP_BODY):
                        load(l, UP_AT + j, i, UP_BODY,
                             a["w_ffn_up"][l, (j % 4) * 512:(j % 4 + 1) * 512,
                                           bass.ds(i * 512 + (j // 4) * D_FF, 512)], (4, 512))
                with sp.Fori(0, KFF // 4) as i:
                    for j in range(4):
                        load(l, DOWN_AT + j, i, 4, a["w_ffn_down"][l, bass.ds(i * 512 + j * P, P), :], (1, D_MODEL))
            sp.wait_ge(x_normed, 2 * NORMS * DEPTH + NORMS)
            sp.dma_start(out[0].rearrange("(m p) c -> p m c", p=P), xt[:, :, :]).then_inc(stored, 16)
            sp.wait_ge(stored, 16)

        @block.gpsimd
        def _(pool):
            for dst, src in ((ident, "c_ident"), (band, "c_band"), (causal, "c_causal")):
                pool.dma_start(dst[:, :], a[src]).then_inc(consts_loaded, 16)
            pool.dma_start(decay[:, :, :], a["c_decay"]).then_inc(consts_loaded, 16)
            for m in range(M):
                pool.dma_start(position[:, m:m + 1],
                               a["positions"][0, m * P:(m + 1) * P].rearrange("(p o) -> p o", o=1)).then_inc(freq_loaded, 16)
            pool.dma_start(freq, a["c_freq"].to_broadcast([P, FREQS])).then_inc(freq_loaded, 16)

            def everywhere(dst, row, signal):
                pool.dma_start(dst, row.to_broadcast([P, row.shape[1]])).then_inc(signal, 16)

            pool.wait_ge(tables_made, 1)
            with pool.Fori(0, DEPTH) as l:
                pool.wait_ge(x_normed, layered(l, 2 * NORMS, NORMS))
                stand_alone(pool)
                pool.dma_start(p_tok, a["p"][l, 0].rearrange("(m p) c -> p m c", p=P)).then_inc(p_loaded, 16)
                everywhere(sinks[:, :], a["attn_sinks"][bass.ds(l, 1), :], sinks_loaded)
                everywhere(vec[:, 0, 0:RET_WIDTH], a["ret_norm_g"][bass.ds(l, 1), :], ret_vec_loaded)
                everywhere(vec[:, 0, RET_WIDTH:], a["ret_norm_b"][bass.ds(l, 1), :], ret_vec_loaded)
                everywhere(vec[:, 1, :], a["ln1_g"][bass.ds(l, 1), :], ln_vec_loaded)
                pool.wait_ge(ret_gated, layered(l, 1, 1))
                stand_alone(pool)
                everywhere(vec[:, 0, :], a["ln1_b"][bass.ds(l, 1), :], ln_vec_loaded)
                for k in range(3):
                    pool.dma_start(conv_rows[0:2 * KFF, k, :],
                                   a["ffn_conv_w"][l, k].rearrange("(c f) -> c f", f=P)).then_inc(conv_loaded, 16)
                pool.dma_start(conv_rows[0:2 * KFF, 3, :],
                               a["ffn_conv_b"][l].rearrange("(c f) -> c f", f=P)).then_inc(conv_loaded, 16)
                pool.wait_ge(x_normed, layered(l, 2 * NORMS, 2 * NORMS))
                stand_alone(pool)
                everywhere(vec[:, 0, :], a["b_ple_gate"][bass.ds(l, 1), :], ple_vec_loaded)
                everywhere(vec[:, 1, :], a["ln2_g"][bass.ds(l, 1), :], ln_vec_loaded)
                pool.wait_ge(ple_sums, layered(l, 4, 4))
                stand_alone(pool)
                everywhere(vec[:, 0, :], a["ln2_b"][bass.ds(l, 1), :], ln_vec_loaded)

        @block.scalar
        def _(act):
            link = Chain(act, act_step)

            def split(l, at, i=0, step=0):
                act.wait_ge(raw_arrived[at % RAW_SLOTS],
                            (layered(l, PANELS // RAW_SLOTS, at // RAW_SLOTS + 1) + i * (step // RAW_SLOTS)) * 16)
                act.wait_ge(panels_used, layered(l, PANELS, at + 1) + i * step)
                nc.scalar.copy(w_hi[:, at % SPLIT_SLOTS, :], raw[:, at % RAW_SLOTS, :]).then_inc(hi_split, 1)

            def used(l, n):
                return layered(l, PANELS, n + SPLIT_SLOTS)

            def take_transposed(l, first):
                for b in range(XT_BANKS):
                    act.wait_ge(transposed, layered(l, T_BANKS, first + b + 1))
                    nc.scalar.copy(xT_hi[:, 2 * b:2 * b + 2, :].rearrange("p k t -> p (k t)"),
                                   ps[:, b, :]).then_inc(xT_hi_done, 1)

            def norm_root(l, first):
                for m in range(M):
                    act.wait_ge(ln_var, layered(l, 2 * M, first + m + 1))
                    nc.scalar.activation(rstd[:, m:m + 1], rstd[:, m:m + 1], ACT.Sqrt).then_inc(ln_std, 1)

            act.sem_inc(proj_copied, 1)
            act.wait_ge(angles_reduced, 2)
            nc.scalar.activation(sine[:, :, :], angle, ACT.Sin)
            nc.scalar.activation(cosine[:, :, :], fine_k, ACT.Sin).then_inc(tables_made, 1)

            with link.loop(DEPTH, 0) as l:
                take_transposed(l, 0)
                act.wait_ge(transposed, layered(l, T_BANKS, XT_BANKS + 1))
                nc.scalar.copy(pT_hi[:, :, :].rearrange("p k t -> p (k t)"), ps[:, 2, :]).then_inc(xT_hi_done, 1)
                split(l, 0)

                for n in range(KV_PANELS):
                    split(l, KV_AT + n + 1)
                act.wait_ge(panels_used, used(l, IN_AT))
                for m in range(M):
                    nc.scalar.copy(proj[:, m, AK:IN_WIDTH], ps[:, m, 0:256]).then_inc(proj_copied, 1)
                with act.Fori(0, IN_LOOPS) as i:
                    for half in range(2):
                        for j in range(4 * half, 4 * half + 4):
                            split(l, IN_AT + j + 1, i, IN_BODY)
                        act.wait_ge(panels_used, used(l, IN_AT + 4 * half + 4) + i * IN_BODY)
                        for m in range(M):
                            nc.scalar.copy(proj[:, m, bass.ds(i * 1024 + half * 512, 512)],
                                           ps[:, 2 - 2 * half + m, :]).then_inc(proj_copied, 1)

                dst = [aqT[:, 2 * n:2 * n + 2] for n in range(4)] + [akT] \
                    + [rqT[:, 2 * n:2 * n + 2] for n in range(4)] + [rkT[:, 2 * n:2 * n + 2] for n in range(4)]
                for n in range(QK_BANKS):
                    act.wait_ge(qk_transposed, layered(l, QK_BANKS, n + 1))
                    nc.scalar.copy(dst[n].rearrange("p c t -> p (c t)"), ps[:, n % 8, :]).then_inc(qk_copied, 1)

                def exponentials(n):
                    u, keys = n % 2, P * (1 + n // 4)
                    act.wait_ge(max_done, layered(l, UNITS, n + 1))
                    for h in range(4):
                        nc.scalar.activation(probs[u][:, h, 0:keys], probs[u][:, h, 0:keys], ACT.Exp,
                                             bias=neg_max[u][:, h:h + 1], accum_out=row_sum[u][:, h:h + 1])
                    nc.scalar.activation(sink_gap[u], sink_gap[u], ACT.Exp).then_inc(exp_done, 1)

                def take_probsT(n):
                    u, kc = n % 2, 1 + n // 4
                    act.wait_ge(probsT_done, layered(l, UNITS, n + 1))
                    for b in range(2):
                        nc.scalar.copy(
                            probsT[u][:, 2 * b:2 * b + 2, 0:kc * P],
                            ps[:, 4 + b, :].rearrange("p (h k) -> p h k", h=2)[:, :, 0:kc * P]).then_inc(probsT_copied, 1)

                def take_attention(n):
                    m, quad = n // 4, n % 4
                    act.wait_ge(att_done, layered(l, UNITS, n + 1))
                    nc.scalar.copy(xT_hi[:, 8 + 2 * quad:10 + 2 * quad, m * P:(m + 1) * P],
                                   ps[:, 6 + n % 2, 0:256].rearrange("p (c t) -> p c t", c=2)).then_inc(att_hi, 1)

                for n in range(UNITS + 2):
                    if n < UNITS:
                        exponentials(n)
                    if 0 <= n - 1 < UNITS:
                        take_probsT(n - 1)
                    if n >= 2:
                        take_attention(n - 2)

                for h in range(RET_HEADS):
                    act.wait_ge(ret_scores_done, layered(l, RET_HEADS, h + 1))
                    nc.scalar.copy(scoresT[h % 2][:, 256:384], ps[:, h % 2, 256:384]).then_inc(ret_cross_copied, 1)
                    act.wait_ge(ret_done, layered(l, RET_HEADS, h + 1))
                    nc.scalar.copy(ret_y[:, :, h * 256:(h + 1) * 256],
                                   ps[:, 2 + h % 2, :].rearrange("p (m c) -> p m c", m=M)).then_inc(ret_copied, 1)
                nc.scalar.activation(ret_sig, proj[:, :, RG:AQ], ACT.Sigmoid).then_inc(ret_sigmoid, 1)
                act.wait_ge(ret_var, layered(l, 1, 1))
                nc.scalar.activation(ret_rstd, ret_rstd, ACT.Sqrt).then_inc(ret_std, 1)
                for b in range(4):
                    act.wait_ge(ret_transposed, layered(l, 4, b + 1))
                    nc.scalar.copy(xT_hi[:, 2 * b:2 * b + 2, :].rearrange("p k t -> p (k t)"),
                                   ps[:, 4 + b, :]).then_inc(ret_hi, 1)

                for n in range(OUT_PANELS):
                    split(l, OUT_AT + n + 1)
                act.wait_ge(conv_transposed, layered(l, 1, 1))
                nc.scalar.copy(conv, ps[:, 0, 0:4 * 2 * KFF].rearrange("p (k c) -> p k c", k=4)).then_inc(conv_copied, 1)
                split(l, PLE_AT + 1)
                norm_root(l, 0)
                split(l, PLE_AT + 2)
                act.wait_ge(panels_used, used(l, GATE_AT))
                for b in PLE_BANKS:
                    nc.scalar.copy(ple[:, b // 4, (b % 4) * BANK:(b % 4 + 1) * BANK], ps[:, b, :]).then_inc(ple_copied, 1)
                take_transposed(l, XT_BANKS + 1)

                for n in range(GATE_PANELS):
                    split(l, GATE_AT + n + 1)

                def begin_conv(half, p, i):
                    if p < 2:
                        act.wait_ge(panels_used, used(l, UP_AT + 4 * half + 4) + i * UP_BODY)
                        act.wait_ge(conv_group_set, layered(l, TAPS, half + 1) + i * 2)
                        for c in (2 * p, 2 * p + 1):
                            if half == 0:
                                dst = work[:, bass.ds(i * (FF_GROUP * SEQ) + c * SEQ, SEQ)]
                            else:
                                dst = tmp[1][:, c * SEQ:(c + 1) * SEQ]
                            last = nc.scalar.activation(
                                dst, ps[:, 2 * half + p, (c % 2) * SEQ:(c % 2 + 1) * SEQ], ACT.Identity,
                                bias=conv_group[:, 3, half, c:c + 1], scale=conv_group[:, 2, half, c:c + 1])
                        last.then_inc(conv_begun, 1)
                    elif p == 2 and half == 0:
                        act.wait_ge(gate_conv, layered(l, FF_GROUPS, 2) + i)
                        stand_alone(act)
                        nc.scalar.activation(tmp[0], work[:, bass.ds(i * (FF_GROUP * SEQ), FF_GROUP * SEQ)],
                                             ACT.Sigmoid).then_inc(gate_sigmoid, 1)

                for n in range(4):
                    split(l, UP_AT + n + 1)
                    act.wait_ge(ple_sums, layered(l, 4, n + 1))
                    nc.scalar.activation(tmp[n % 2], tmp[n % 2], ACT.Sigmoid).then_inc(ple_sigmoid, 1)
                with act.Fori(0, FF_GROUPS - 1) as i:
                    for j in range(UP_BODY):
                        split(l, UP_AT + 4 + j + 1, i, UP_BODY)
                        begin_conv(j // 4, j % 4, i)

                def down_step(j, i):
                    split(l, DOWN_AT + j, i, 4)
                    act.wait_ge(panels_used, used(l, DOWN_AT + j - 3) + i * 4)
                    nc.scalar.copy(xT_hi[:, j % 4, :], work[:, bass.ds(i * (4 * SEQ) + j * SEQ, SEQ)]).then_inc(g_hi, 1)

                for j in range(4):
                    if j < 3:
                        split(l, DOWN_AT - 4 + j + 1)
                    else:
                        down_step(0, 0)
                    begin_conv(0, j, FF_GROUPS - 1)

                for j in range(4):
                    down_step(j + 1, 0)
                    if j == 0:
                        begin_conv(1, 0, FF_GROUPS - 1)
                        begin_conv(1, 1, FF_GROUPS - 1)
                with act.Fori(1, KFF // 4 - 1) as i:
                    for j in range(4):
                        down_step(j + 1, i)
                for j in range(3):
                    down_step(j + 1, KFF // 4 - 1)
                norm_root(l, M)

        @block.vector
        def _(dve):
            link = Chain(dve, dve_step)
            tt, ts, stt = nc.vector.tensor_tensor, nc.vector.tensor_scalar, nc.vector.scalar_tensor_tensor

            def used(l, n):
                return layered(l, PANELS, n + SPLIT_SLOTS)

            def split(l, at, i=0, step=0):
                dve.wait_ge(hi_split, layered(l, PANELS, at + 1) + i * step)
                tt(w_lo[:, at % SPLIT_SLOTS, :], raw[:, at % RAW_SLOTS, :],
                   w_hi[:, at % SPLIT_SLOTS, :].bitcast(F32), ALU.subtract).then_inc(panels_split, 1)

            def take_transposed(l, first):
                for b in range(XT_BANKS):
                    dve.wait_ge(xT_hi_done, layered(l, T_BANKS, first + b + 1))
                    tt(xT_lo[:, 2 * b:2 * b + 2, :].rearrange("p k t -> p (k t)"), ps[:, b, :],
                       xT_hi[:, 2 * b:2 * b + 2, :].rearrange("p k t -> p (k t)").bitcast(F32),
                       ALU.subtract).then_inc(xT_lo_done, 1)

            def add_and_norm(l, products, factor, norm, between=lambda: None):
                dve.wait_ge(panels_used, used(l, products))
                for b in range(8):
                    part = xt[:, b // 4, (b % 4) * BANK:(b % 4 + 1) * BANK]
                    stt(part, part, factor, ps[:, b, :], ALU.mult, ALU.add).then_inc(sums_taken, 1)
                between()
                for m in range(M):
                    dve.wait_ge(sums_taken, layered(l, 16, 8 * norm + 4 * m + 4))
                    for n in range(4):
                        last = nc.vector.bn_stats(stats[:, m, 6 * n:6 * n + 6], xt[:, m, n * BANK:(n + 1) * BANK])
                    link(last)
                    stand_alone(dve)
                    link(nc.vector.bn_aggr(moments[:, m, :], stats[:, m, :]))
                    ts(rstd[:, m:m + 1], moments[:, m, 1:2], LN_EPS, None, ALU.add).then_inc(ln_var, 1)
                for m in range(M):
                    dve.wait_ge(ln_std, layered(l, 2 * M, norm * M + m + 1))
                    link(nc.vector.reciprocal(rstd[:, m:m + 1], rstd[:, m:m + 1]))
                dve.wait_ge(ln_vec_loaded, layered(l, 64, 32 * (1 + norm)))
                for part in range(NORMS):
                    m, cols = part % M, slice(part // M * 1024, part // M * 1024 + 1024)
                    x = xt[:, m, cols]
                    link(stt(x, x, moments[:, m, 0:1], vec[:, 1, cols], ALU.subtract, ALU.mult))
                    stt(x, x, rstd[:, m:m + 1], vec[:, 0, cols], ALU.mult, ALU.add).then_inc(x_normed, 1)

            def rotate(heads, table, m):
                n, half = heads.shape[1], heads.shape[3]
                x1, x2 = heads[:, :, 0, :], heads[:, :, 1, :]
                cos = cosine[:, m, table:table + half].unsqueeze(1).to_broadcast([P, n, half])
                sin = sine[:, m, table:table + half].unsqueeze(1).to_broadcast([P, n, half])
                x1_sin = rot_a[:, 0:n * half].rearrange("p (h f) -> p h f", h=n)
                x2_sin = rot_b[:, 0:n * half].rearrange("p (h f) -> p h f", h=n)
                tt(x1_sin, x1, sin, ALU.mult)
                link(tt(x2_sin, x2, sin, ALU.mult))
                tt(x1, x1, cos, ALU.mult)
                link(tt(x2, x2, cos, ALU.mult))
                tt(x1, x1, x2_sin, ALU.subtract)
                link(tt(x2, x2, x1_sin, ALU.add))

            dve.sem_inc(panels_split, RAW_SLOTS)
            dve.sem_inc(gate_conv, 1)
            dve.sem_inc(up_taken, 1)
            dve.sem_inc(x_normed, NORMS)

            dve.wait_ge(freq_loaded, 16 * (M + 1))
            link(nc.vector.tensor_copy(position_f[:, :], position[:, :]))
            for m in range(M):
                last = ts(angle[:, m, :], freq, position_f[:, m:m + 1], None, ALU.mult)
            link(last)

            def turns(dst, src, turn):
                link(ts(dst, src, 1.0 / turn, ROUND, ALU.mult, ALU.add))
                link(ts(dst, dst, ROUND, None, ALU.subtract))

            def less(k, part):
                link(stt(angle, k, -part, angle, ALU.mult, ALU.add))

            turns(coarse_k, angle, 2.0 * np.pi * PERIODS)
            for part in COARSE[0:3]:
                less(coarse_k, part)
            link(stt(fine_k, coarse_k, -COARSE[3], angle, ALU.mult, ALU.add))
            turns(fine_k, fine_k, 2.0 * np.pi)
            for k, part in ((fine_k, FINE[0]), (coarse_k, COARSE[3]), (fine_k, FINE[1]), (coarse_k, COARSE[4]),
                            (fine_k, FINE[2]), (coarse_k, COARSE[5]), (coarse_k, COARSE[6])):
                less(k, part)
            pi = float(np.nextafter(np.float32(np.pi), np.float32(0)))
            link(ts(angle, angle, pi, -pi, ALU.min, ALU.max))
            link(stt(fine_k, angle, -1.0, angle, ALU.mult, ALU.max))
            ts(fine_k, fine_k, -1.0, float(np.pi / 2), ALU.mult, ALU.add).then_inc(angles_reduced, 2)

            with link.loop(DEPTH, LINKS) as l:
                take_transposed(l, 0)
                dve.wait_ge(xT_hi_done, layered(l, T_BANKS, XT_BANKS + 1))
                tt(pT_lo[:, :, :].rearrange("p k t -> p (k t)"), ps[:, 2, :],
                   pT_hi[:, :, :].rearrange("p k t -> p (k t)").bitcast(F32), ALU.subtract).then_inc(xT_lo_done, 1)
                split(l, 0)
                for n in range(KV_PANELS):
                    split(l, KV_AT + n + 1)
                stand_alone(dve)
                with dve.Fori(0, IN_LOOPS) as i:
                    for j in range(IN_BODY):
                        split(l, IN_AT + j + 1, i, IN_BODY)

                dve.wait_ge(tables_made, 1)
                dve.wait_ge(consts_loaded, 64)
                dve.wait_ge(proj_copied, layered(l, COPIES, COPIES + 1))
                for m in range(M):
                    rotate(proj[:, m, AQ:AV].rearrange("p (h e f) -> p h e f", e=2, f=ATT_DIM // 2), RET_DIM // 2, m)
                    for kv in range(ATT_KV):
                        k = proj[:, m, AK + kv * ATT_DIM:AK + (kv + 1) * ATT_DIM]
                        last = nc.vector.tensor_copy(k_twice[:, m, kv, :, :],
                                                     k.unsqueeze(1).to_broadcast([P, 2, ATT_DIM]))
                    link(last)
                for m in range(M):
                    rotate(proj[:, m, RQ:RV].rearrange("p (h e f) -> p h e f", e=2, f=RET_DIM // 2), 0, m)
                    heads = proj[:, m, RQ:RV].rearrange("p (h c) -> p h c", c=RET_DIM)
                    link(tt(heads, heads, decay[:, m, :].unsqueeze(2).to_broadcast([P, 2 * RET_HEADS, RET_DIM]),
                            ALU.mult))
                dve.sem_inc(rotated, 1)

                dve.wait_ge(sinks_loaded, layered(l, 16, 16))

                def maxima(n):
                    u, quad, keys = n % 2, n % 4, P * (1 + n // 4)
                    mask = (band[:, P:] if n < 4 else band[:, :]).unsqueeze(1).to_broadcast([P, 2, keys])
                    dve.wait_ge(scores_done, layered(l, UNITS, n + 1))
                    if n >= 2:
                        dve.wait_ge(probsT_done, layered(l, UNITS, n - 1))
                    for e in range(2):
                        scores = ps[:, 2 * u + e, :].rearrange("p (c k) -> p c k", c=2)[:, :, 0:keys]
                        last = stt(probs[u].rearrange("p (c e) k -> p e c k", e=2)[:, e, :, 0:keys], scores,
                                   ATT_DIM ** -0.5, mask, ALU.mult, ALU.add)
                    link(last)
                    sink = sinks[:, 4 * quad:4 * quad + 4]
                    link(nc.vector.reduce_max(row_max[u], probs[u][:, :, 0:keys], AX_X))
                    link(tt(row_max[u], row_max[u], sink, ALU.max))
                    ts(neg_max[u], row_max[u], -1.0, None, ALU.mult)
                    tt(sink_gap[u], sink, row_max[u], ALU.subtract).then_inc(max_done, 1)

                def normalise(n):
                    u, keys = n % 2, P * (1 + n // 4)
                    dve.wait_ge(exp_done, layered(l, UNITS, n + 1))
                    link(tt(row_sum[u], row_sum[u], sink_gap[u], ALU.add))
                    link(nc.vector.reciprocal(row_sum[u], row_sum[u]))
                    p = probs[u][:, :, 0:keys]
                    tt(p, p, row_sum[u].unsqueeze(2).to_broadcast([P, 4, keys]), ALU.mult).then_inc(probs_done, 1)

                def take_attention(n):
                    m, quad = n // 4, n % 4
                    dve.wait_ge(att_hi, layered(l, UNITS, n + 1))
                    part = (slice(None), slice(8 + 2 * quad, 10 + 2 * quad), slice(m * P, (m + 1) * P))
                    tt(xT_lo[part], ps[:, 6 + n % 2, 0:256].rearrange("p (c t) -> p c t", c=2),
                       xT_hi[part].bitcast(F32), ALU.subtract).then_inc(att_lo, 1)

                maxima(0)
                for n in range(UNITS):
                    if n + 1 < UNITS:
                        maxima(n + 1)
                    normalise(n)
                    if n >= 2:
                        take_attention(n - 2)
                for n in (UNITS - 2, UNITS - 1):
                    take_attention(n)

                for h in range(RET_HEADS):
                    dve.wait_ge(ret_cross_copied, layered(l, RET_HEADS, h + 1))
                    tt(scoresT[h % 2][:, 0:256].rearrange("p (b t) -> p b t", b=2),
                       ps[:, h % 2, 0:256].rearrange("p (b t) -> p b t", b=2),
                       causal[:, :].unsqueeze(1).to_broadcast([P, 2, P]), ALU.mult).then_inc(ret_scores_masked, 1)
                for h in range(RET_HEADS):
                    dve.wait_ge(ret_copied, layered(l, RET_HEADS, h + 1))
                    for m in range(M):
                        link(nc.vector.bn_stats(ret_stats, ret_y[:, m, h * RET_DIM:(h + 1) * RET_DIM]))
                        stand_alone(dve)
                        link(nc.vector.bn_aggr(ret_moments[:, m, h, :], ret_stats))
                ts(ret_rstd, ret_moments[:, :, :, 1], GN_EPS, None, ALU.add).then_inc(ret_var, 1)
                dve.wait_ge(ret_sigmoid, layered(l, 1, 1))
                link(tt(ret_sig, ret_sig, proj[:, :, RG:AQ], ALU.mult))
                dve.wait_ge(ret_std, layered(l, 1, 1))
                link(nc.vector.reciprocal(ret_rstd, ret_rstd))
                for m in range(M):
                    for h in range(RET_HEADS):
                        y = ret_y[:, m, h * RET_DIM:(h + 1) * RET_DIM]
                        last = ts(y, y, ret_moments[:, m, h, 0:1], ret_rstd[:, m, h:h + 1], ALU.subtract, ALU.mult)
                link(last)
                dve.wait_ge(ret_vec_loaded, layered(l, 32, 32))
                for v, op in ((vec[:, 0, 0:RET_WIDTH], ALU.mult), (vec[:, 0, RET_WIDTH:], ALU.add)):
                    link(tt(ret_y, ret_y, v.unsqueeze(1).to_broadcast([P, M, RET_WIDTH]), op))
                tt(ret_y, ret_y, ret_sig, ALU.mult).then_inc(ret_gated, 1)
                for b in range(4):
                    dve.wait_ge(ret_hi, layered(l, 4, b + 1))
                    tt(xT_lo[:, 2 * b:2 * b + 2, :].rearrange("p k t -> p (k t)"), ps[:, 4 + b, :],
                       xT_hi[:, 2 * b:2 * b + 2, :].rearrange("p k t -> p (k t)").bitcast(F32),
                       ALU.subtract).then_inc(ret_lo, 1)

                for n in range(OUT_PANELS):
                    split(l, OUT_AT + n + 1)
                add_and_norm(l, PLE_AT, ALPHA, 0, lambda: split(l, PLE_AT + 1))
                split(l, PLE_AT + 2)
                take_transposed(l, XT_BANKS + 1)

                for n in range(GATE_PANELS):
                    split(l, GATE_AT + n + 1)

                def set_taps(half, i):
                    link(nc.vector.tensor_copy(conv_group[:, :, half, :],
                                               conv[:, :, bass.ds(i * FF_GROUP + half * KFF, FF_GROUP)]))
                    dve.sem_inc(conv_group_set, 1)

                def convolve(half, p, i):
                    group = work[:, bass.ds(i * (FF_GROUP * SEQ), FF_GROUP * SEQ)]
                    if p < 2:
                        dve.wait_ge(conv_begun, layered(l, 4 * FF_GROUPS, 2 * half + p + 1) + i * 4)
                        for back in (1, 2):
                            for c in (2 * p, 2 * p + 1):
                                u = ps[:, 2 * half + p, (c % 2) * SEQ:(c % 2 + 1) * SEQ - back]
                                if half == 0:
                                    dst = work[:, bass.ds(i * (FF_GROUP * SEQ) + c * SEQ + back, SEQ - back)]
                                else:
                                    dst = tmp[1][:, c * SEQ + back:(c + 1) * SEQ]
                                last = stt(dst, u, conv_group[:, 2 - back, half, c:c + 1], dst, ALU.mult, ALU.add)
                            link(last)
                        if p == 1:
                            dve.sem_inc((gate_conv, up_taken)[half], 1)
                    elif p == 2:
                        if half == 0:
                            dve.wait_ge(gate_sigmoid, layered(l, FF_GROUPS, 1) + i)
                        link(tt(group, group, tmp[half], ALU.mult))
                    else:
                        set_taps(1 - half, i + half)

                dve.wait_ge(conv_copied, layered(l, 1, 1))
                set_taps(0, 0)
                dve.wait_ge(ple_vec_loaded, layered(l, 16, 16))

                def finish_ple(n):
                    m, cols = n // 2, slice((n % 2) * 1024, (n % 2 + 1) * 1024)
                    dve.wait_ge(ple_sigmoid, layered(l, 4, n + 1))
                    link(tt(ple[:, m, cols], ple[:, m, cols], tmp[n % 2], ALU.mult))
                    link(stt(xt[:, m, cols], xt[:, m, cols], ALPHA, ple[:, m, cols], ALU.mult, ALU.add))

                for n in range(4):
                    split(l, UP_AT + n + 1)
                    m, cols = n // 2, slice((n % 2) * 1024, (n % 2 + 1) * 1024)
                    if n == 0:
                        dve.wait_ge(panels_used, used(l, UP_AT))
                    if n >= 2:
                        finish_ple(n - 2)
                    tt(tmp[n % 2].rearrange("p (b c) -> p b c", b=2), ps[:, 2 * n:2 * n + 2, :],
                       vec[:, 0, cols].rearrange("p (b c) -> p b c", b=2), ALU.add).then_inc(ple_sums, 1)
                finish_ple(2)
                finish_ple(3)
                stand_alone(dve)
                with link.loop(FF_GROUPS - 1, UP_LINKS) as i:
                    for j in range(UP_BODY):
                        split(l, UP_AT + 4 + j + 1, i, UP_BODY)
                        convolve(j // 4, j % 4, i)

                def down_step(j, i):
                    split(l, DOWN_AT + j, i, 4)
                    dve.wait_ge(g_hi, layered(l, KFF, j + 1) + i * 4)
                    tt(xT_lo[:, j % 4, :], work[:, bass.ds(i * (4 * SEQ) + j * SEQ, SEQ)],
                       xT_hi[:, j % 4, :].bitcast(F32), ALU.subtract).then_inc(g_split, 1)

                for j in range(4):
                    if j < 3:
                        split(l, DOWN_AT - 4 + j + 1)
                    else:
                        down_step(0, 0)
                    convolve(0, j, FF_GROUPS - 1)

                for j in range(4):
                    down_step(j + 1, 0)
                    if j == 0:
                        convolve(1, 0, FF_GROUPS - 1)
                        convolve(1, 1, FF_GROUPS - 1)
                    if j == 1:
                        convolve(1, 2, FF_GROUPS - 1)
                stand_alone(dve)
                with dve.Fori(1, KFF // 4 - 1) as i:
                    for j in range(4):
                        down_step(j + 1, i)
                for j in range(3):
                    down_step(j + 1, KFF // 4 - 1)
                add_and_norm(l, PANELS, 1.0, 1)

        @block.tensor
        def _(pe):
            mm = nc.tensor.matmul

            def panel(l, at, i, step, products):
                pe.wait_ge(panels_split, layered(l, PANELS, at + 1 + RAW_SLOTS) + i * step)
                for bank, hi, lo, x_hi, x_lo, first, last, flip, wait in products:
                    if wait:
                        pe.wait_ge(*wait)
                    pairs = ((x_hi, lo), (x_hi, hi), (x_lo, hi))
                    for n, (x, w) in enumerate(pairs):
                        lhs, rhs = (w, x) if flip else (x, w)
                        done = mm(bank, lhs, rhs, start=first and n == 0, stop=last and n == 2,
                                  skip_group_check=flip)
                done.then_inc(panels_used, 1)

            def tokens_by_columns(s, k_chunks, width, x_slots, banks, first, last, xh=xT_hi, xl=xT_lo,
                                  order=None, waits={}):
                order = order or [(m, n) for m in range(M) for n in range((width + BANK - 1) // BANK)]
                found = []
                for k in range(k_chunks):
                    for m, n in order:
                        lo, hi = k * width + n * BANK, k * width + min(width, (n + 1) * BANK)
                        x = (slice(None), x_slots[k], slice(m * P, (m + 1) * P))
                        found.append((banks(m, n)[:, 0:hi - lo], w_hi[:, s, lo:hi], w_lo[:, s, lo:hi], xh[x], xl[x],
                                      first and k == 0, last and k == k_chunks - 1, False, waits.get((m, n))))
                return found

            def transpose(dst, src):
                return nc.tensor.transpose(dst, src, ident[:, :])

            def transpose_x(l, norm):
                for b in range(XT_BANKS):
                    if b % 4 == 0:
                        pe.wait_ge(x_normed, layered(l, 2 * NORMS, NORMS * norm + (b // 4 + 1) * M))
                    if norm == 1:
                        pe.wait_ge(ple_copied, layered(l, 8, PLE_BANKS.index(b) + 1))
                    for k in (2 * b, 2 * b + 1):
                        for m in range(M):
                            col = (k % 2) * SEQ + m * P
                            last = transpose(ps[:, b, col:col + P], xt[:, m, k * P:(k + 1) * P])
                    last.then_inc(transposed, 1)

            def wide(l, at, slot, first, last, i=0, step=0, xh=xT_hi, xl=xT_lo, order=None, waits={}):
                panel(l, at, i, step,
                      tokens_by_columns(at % SPLIT_SLOTS, 1, D_MODEL, [slot], lambda m, n: ps[:, 4 * m + n, :],
                                        first, last, xh, xl, order, waits))

            pe.sem_inc(panels_used, SPLIT_SLOTS)
            pe.wait_ge(x_loaded, 16)
            pe.wait_ge(consts_loaded, 64)

            with pe.Fori(0, DEPTH) as l:
                transpose_x(l, 0)
                pe.wait_ge(p_loaded, layered(l, 16, 16))
                pe.wait_ge(xT_lo_done, layered(l, T_BANKS, 3))
                for k in range(PLE_PANELS):
                    for m in range(M):
                        last = transpose(ps[:, 2, k * SEQ + m * P:k * SEQ + (m + 1) * P], p_tok[:, m, k * P:(k + 1) * P])
                last.then_inc(transposed, 1)

                for n in range(KV_PANELS):
                    pe.wait_ge(xT_lo_done, layered(l, T_BANKS, 4 if n == 0 else XT_BANKS + 1))
                    panel(l, KV_AT + n, 0, 0,
                          tokens_by_columns((KV_AT + n) % SPLIT_SLOTS, 8, 256, range(8 * n, 8 * n + 8),
                                            lambda m, n: ps[:, m, :], n == 0, n == 1))
                with pe.Fori(0, IN_LOOPS) as i:
                    for half in range(2):
                        pe.wait_ge(proj_copied, layered(l, COPIES, 2 * half + 1) + i * 4)
                        for j in range(4):
                            at = IN_AT + 4 * half + j
                            panel(l, at, i, IN_BODY,
                                  tokens_by_columns(at % SPLIT_SLOTS, 4, 512, range(4 * j, 4 * j + 4),
                                                    lambda m, n: ps[:, 2 - 2 * half + m, :], j == 0, j == 3))

                pe.wait_ge(rotated, layered(l, 1, 1))
                pe.wait_ge(proj_copied, layered(l, COPIES, COPIES + 1))
                sources = [[[proj[:, m, AQ + c * P:AQ + (c + 1) * P] for m in range(M)] for c in range(8)],
                           [[k_twice[:, m, kv, :, :].rearrange("p e d -> p (e d)") for m in range(M)]
                            for kv in range(ATT_KV)],
                           [[proj[:, m, c * P:(c + 1) * P] for m in range(M)] for c in range(16)]]
                chunks = [c for s in sources for c in s]
                for n in range(QK_BANKS):
                    if n == 0:
                        pass
                    if n >= 8:
                        pe.wait_ge(qk_copied, layered(l, QK_BANKS, n - 7))
                    for c in (0, 1):
                        for m in range(M):
                            last = transpose(ps[:, n % 8, c * SEQ + m * P:c * SEQ + (m + 1) * P], chunks[2 * n + c][m])
                    last.then_inc(qk_transposed, 1)
                pe.wait_ge(qk_copied, layered(l, QK_BANKS, QK_BANKS))

                def scores(n):
                    m, quad, u, keys = n // 4, n % 4, n % 2, P * (1 + n // 4)
                    if n >= 2:
                        pe.wait_ge(max_done, layered(l, UNITS, n - 1))
                    for c in range(2):
                        for e in range(2):
                            half = slice(64 * e, 64 * e + 64)
                            last = mm(ps[:, 2 * u + e, c * 256:c * 256 + keys],
                                      aqT[half, 2 * quad + c, m * P:(m + 1) * P],
                                      akT[half, quad // 2, 0:keys], start=True, stop=True)
                    last.then_inc(scores_done, 1)

                def transpose_probs(n):
                    u, kc = n % 2, 1 + n // 4
                    pe.wait_ge(probs_done, layered(l, UNITS, n + 1))
                    if n >= 1:
                        pe.wait_ge(probsT_copied, layered(l, 2 * UNITS, 2 * n))
                    for h in range(4):
                        for k in range(kc):
                            col = (h % 2) * 256 + k * P
                            last = transpose(ps[:, 4 + h // 2, col:col + P], probs[u][:, h, k * P:(k + 1) * P])
                    last.then_inc(probsT_done, 1)

                def attend(n):
                    quad, u, kc = n % 4, n % 2, 1 + n // 4
                    pe.wait_ge(probsT_copied, layered(l, 2 * UNITS, 2 * n + 2))
                    if n >= 2:
                        pe.wait_ge(att_lo, layered(l, UNITS, n - 1))
                    v = slice(AV + (quad // 2) * ATT_DIM, AV + (quad // 2 + 1) * ATT_DIM)
                    for c in range(2):
                        for e in range(2):
                            for k in range(kc):
                                last = mm(ps[64 * e:64 * e + 64, 6 + n % 2, c * P:(c + 1) * P], proj[:, k, v],
                                          probsT[u][:, 2 * c + e, k * P:(k + 1) * P], start=k == 0, stop=k == kc - 1)
                    last.then_inc(att_done, 1)

                scores(0)
                scores(1)
                for n in range(UNITS):
                    transpose_probs(n)
                    if n + 2 < UNITS:
                        scores(n + 2)
                    attend(n)

                pe.wait_ge(att_lo, layered(l, UNITS, UNITS))

                def ret_scores(h):
                    if h >= 2:
                        pe.wait_ge(ret_scores_masked, layered(l, RET_HEADS, h - 1))
                    for col, j, i in ((0, 0, 0), (P, 1, 1), (2 * P, 0, 1)):
                        for k in range(2):
                            last = mm(ps[:, h % 2, col:col + P], rkT[:, 2 * h + k, j * P:(j + 1) * P],
                                      rqT[:, 2 * h + k, i * P:(i + 1) * P], start=k == 0, stop=k == 1)
                    last.then_inc(ret_scores_done, 1)

                ret_scores(0)
                ret_scores(1)
                for h in range(RET_HEADS):
                    pe.wait_ge(ret_scores_masked, layered(l, RET_HEADS, h + 1))
                    if h >= 2:
                        pe.wait_ge(ret_copied, layered(l, RET_HEADS, h - 1))
                    s, cols = scoresT[h % 2], slice(RV + h * RET_DIM, RV + (h + 1) * RET_DIM)
                    y = ps[:, 2 + h % 2, :].rearrange("p (m c) -> p m c", m=M)
                    mm(y[:, 0, :], s[:, 0:P], proj[:, 0, cols], start=True, stop=True)
                    mm(y[:, 1, :], s[:, 2 * P:3 * P], proj[:, 0, cols], start=True, stop=False)
                    mm(y[:, 1, :], s[:, P:2 * P], proj[:, 1, cols], start=False, stop=True).then_inc(ret_done, 1)
                    if h + 2 < RET_HEADS:
                        ret_scores(h + 2)
                pe.wait_ge(ret_gated, layered(l, 1, 1))
                for b in range(4):
                    for c in (0, 1):
                        for m in range(M):
                            last = transpose(ps[:, 4 + b, c * SEQ + m * P:c * SEQ + (m + 1) * P],
                                             ret_y[:, m, (2 * b + c) * P:(2 * b + c + 1) * P])
                    last.then_inc(ret_transposed, 1)

                pe.wait_ge(ret_lo, layered(l, 4, 4))
                for n in range(OUT_PANELS):
                    wide(l, OUT_AT + n, n, n == 0, n == OUT_PANELS - 1)

                pe.wait_ge(conv_loaded, layered(l, 64, 64))
                pe.wait_ge(sums_taken, layered(l, 16, 1))
                for k in range(4):
                    last = nc.tensor.transpose(ps[:, 0, k * 2 * KFF:(k + 1) * 2 * KFF], conv_rows[0:2 * KFF, k, :],
                                               ident[0:2 * KFF, 0:2 * KFF])
                last.then_inc(conv_transposed, 1)

                order = [(b // 4, b % 4) for b in PLE_BANKS]
                waits = {(b // 4, b % 4): (sums_taken, layered(l, 16, b + 1)) for b in PLE_BANKS if b}
                waits[0, 0] = (conv_copied, layered(l, 1, 1))
                for n in range(PLE_PANELS):
                    wide(l, PLE_AT + n, n, n == 0, n == PLE_PANELS - 1, xh=pT_hi, xl=pT_lo, order=order,
                         waits=waits if n == 0 else {})

                transpose_x(l, 1)
                pe.wait_ge(xT_lo_done, layered(l, T_BANKS, T_BANKS))
                for n in range(GATE_PANELS):
                    wide(l, GATE_AT + n, n, n == 0, n == GATE_PANELS - 1)

                with pe.Fori(0, FF_GROUPS) as i:
                    for half in range(2):
                        pe.wait_ge(ple_sums, layered(l, 4, half + 1))
                        pe.wait_ge((gate_conv, up_taken)[half], layered(l, FF_GROUPS, 1) + i)
                        for j in range(4):
                            at = UP_AT + 4 * half + j
                            s = at % SPLIT_SLOTS
                            products = []
                            for k in range(4):
                                for c in range(FF_GROUP):
                                    w = slice(k * 512 + c * P, k * 512 + (c + 1) * P)
                                    products.append((ps[:, 2 * half + c // 2, (c % 2) * SEQ:(c % 2 + 1) * SEQ],
                                                     w_hi[:, s, w], w_lo[:, s, w],
                                                     xT_hi[:, 4 * j + k, :], xT_lo[:, 4 * j + k, :],
                                                     j == 0 and k == 0 and c % 2 == 0, j == 3 and k == 3, True, None))
                            panel(l, at, i, UP_BODY, products)

                pe.wait_ge(ple_sums, layered(l, 4, 4))
                order = [(1, n) for n in range(4)] + [(0, n) for n in range(4)]
                waits = {(0, 0): (gate_conv, layered(l, FF_GROUPS, FF_GROUPS + 1)),
                         (0, 2): (up_taken, layered(l, FF_GROUPS, FF_GROUPS + 1))}

                def down(j, i, first=False, last=False, waits={}):
                    pe.wait_ge(g_split, layered(l, KFF, j + 1) + i * 4)
                    wide(l, DOWN_AT + j, j, first, last, i=i, step=4, order=order, waits=waits)

                down(0, 0, first=True, waits=waits)
                for j in range(1, 4):
                    down(j, 0)
                with pe.Fori(1, KFF // 4 - 1) as i:
                    for j in range(4):
                        down(j, i)
                for j in range(4):
                    down(j, KFF // 4 - 1, last=j == 3)


UP_LINKS = 2 * (2 * 2 + 1 + 1)
LINKS = 2 * M * 4 + UNITS * 5 + 2 * RET_HEADS * M + 5 + 2 * (3 * M + NORMS) + 1 + 8 + FF_GROUPS * UP_LINKS - 1


def constants():
    f = np.float32
    ret = f(1.0) / np.power(f(10000.0), np.linspace(0.0, 1.0, RET_DIM // 2, dtype=f))
    att = np.power(f(10000.0), -np.arange(0, ATT_DIM, 2, dtype=f) / f(ATT_DIM))
    i = np.arange(P)
    later = i[:, None] >= i[None, :]
    band = np.where(np.concatenate([~later, later], 1), 0.0, MASKED)
    gamma = np.log1p(-np.exp2(-5.0 - np.arange(RET_HEADS)))
    t = (np.arange(SEQ) - SEQ // 2)[:, None]
    decay = np.concatenate([np.exp(gamma * t), np.exp(-gamma * t) * RET_DIM ** -0.5], 1)
    return {
        "c_freq": np.concatenate([ret, att])[None, :].astype(f),
        "c_ident": np.eye(P, dtype=f),
        "c_band": band.astype(f),
        "c_causal": (i[:, None] <= i[None, :]).astype(f),
        "c_decay": np.ascontiguousarray(decay.reshape(M, P, 2 * RET_HEADS).transpose(1, 0, 2)).astype(f),
    }


def kernel(**inputs):
    import concourse.bacc as bacc
    from concourse.bass_utils import run_bass_kernel_spmd

    nc = bacc.Bacc("TRN2", target_bir_lowering=False, num_devices=1)
    arrays, aps = {}, {}
    for name, value in [*inputs.items(), *constants().items()]:
        value = np.ascontiguousarray(value)
        arrays[f"in_{name}"] = value
        aps[name] = nc.dram_tensor(f"in_{name}", value.shape, mybir.dt.from_np(value.dtype), kind="ExternalInput").ap()
    out = nc.dram_tensor("out_x", (1, SEQ, D_MODEL), F32, kind="ExternalOutput").ap()
    build(nc, aps, out)
    result = run_bass_kernel_spmd(nc, [arrays], core_ids=[0])
    return result.results[0]["out_x"]
```

```python
from contextlib import ExitStack, contextmanager

import numpy as np
import concourse.bass as bass
from concourse import mybir

F32 = mybir.dt.float32
F32R = mybir.dt.float32r
I32 = mybir.dt.int32
ALU = mybir.AluOpType
ACT = mybir.ActivationFunctionType
AX_X = mybir.AxisListType.X

P = 128
D_MODEL, SEQ, DEPTH, PLE_DIM = 2048, 256, 2, 256
D_FF = 5632
M = SEQ // P
KD = D_MODEL // P
RET_HEADS, RET_DIM = 4, 256
RET_WIDTH = RET_HEADS * RET_DIM
ATT_HEADS, ATT_KV, ATT_DIM = 16, 2, 64
ATT_WIDTH = ATT_HEADS * ATT_DIM
RQ, RK, RV, RG, AQ = (n * RET_WIDTH for n in range(5))
AK = AQ + ATT_WIDTH
AV = AK + ATT_KV * ATT_DIM
IN_WIDTH = AV + ATT_KV * ATT_DIM
FREQS = RET_DIM // 2 + ATT_DIM // 2
ALPHA = float((2 * DEPTH) ** 0.25)
LN_EPS, GN_EPS = 1e-5, 1e-6
MASKED = -3.0e38

PANEL = 2048
RAW_SLOTS, SPLIT_SLOTS = 4, 2
BANK = 512
FF_GROUP = 4
FF_GROUPS = D_FF // P // FF_GROUP
KFF = D_FF // P

KV_PANELS = 2
HALF_PANELS = 4
OUT_PANELS = KD
PLE_PANELS = PLE_DIM // P
UP_BODY = 8
GATE_PANELS = KD
KV_AT = 0
IN_AT = KV_AT + KV_PANELS
OUT_AT = IN_AT + AK // 512 * HALF_PANELS
PLE_AT = OUT_AT + OUT_PANELS
GATE_AT = PLE_AT + PLE_PANELS
UP_AT = GATE_AT + GATE_PANELS
DOWN_AT = UP_AT + FF_GROUPS * UP_BODY
PANELS = DOWN_AT + KFF

COPIES = M * (1 + AK // 512)
XT_BANKS = KD // 2
T_BANKS = 2 * XT_BANKS + 1
AQK_BANKS = 5
UNITS = M * ATT_KV * 2
TAPS = 2 * FF_GROUPS
BANKS_MADE = 3 * 7


HALVES = [first + n for first in (AQ, RQ, RK, RG, RV) for n in (0, 512)]

STEPS = OUT_AT - IN_AT + 8
AQ_MADE, RQ_MADE, RK_MADE, RG_MADE, RV_MADE = (HALF_PANELS * 2 * n for n in range(1, 6))
AQK_TRANSPOSE = {AQ_MADE + 2: (0, 1), AQ_MADE + 3: (2, 3), AQ_MADE + 4: (4,)}
AQK_PSUM = (4, 5, 6, 7, 6)
UNIT_START = AQ_MADE + 4
SCORES, MAXIMA, EXPONENTIALS, NORMALISE, TRANSPOSE_P, TAKE_P, ATTEND, TAKE_O = 0, 1, 2, 3, 3, 4, 4, 5
RQK_TRANSPOSE = {RG_MADE - 4: (0, 1), RG_MADE - 3: (4, 5), RG_MADE - 2: (2, 3), RG_MADE - 1: (6, 7)}
RET_SCORES = RG_MADE
SILU = RG_MADE + 1
RET_PV = (RG_MADE + 4, RV_MADE)


RQK_ORDER = [n for pair in RQK_TRANSPOSE.values() for n in pair]
RET_PSUM = (2, 3, 6, 7)


def unit(s, stage):
    n, odd = divmod(s - UNIT_START - stage, 2)
    return n if not odd and 0 <= n < UNITS else None


def layered(l, per_layer, n):
    return l * per_layer + n


class Chain:

    def __init__(self, eng, sem):
        self.eng, self.sem, self.base, self.n = eng, sem, 0, 0

    def __call__(self, instruction):
        instruction.then_inc(self.sem, 1)
        self.n += 1
        self.eng.wait_ge(self.sem, self.base + self.n)

    @contextmanager
    def loop(self, count, links):
        base, first = self.base, self.n
        with self.eng.Fori(0, count) as i:
            self.base = base + i * links
            yield i
            assert self.n - first == links, (self.n - first, links)
        self.base, self.n = base, first + count * links


PLE_BANKS = (1, 2, 3, 4, 5, 6, 7, 0)
P_PSUM = 6
XT_PSUM = (tuple(range(XT_BANKS)), PLE_BANKS)
SCALE = 160
TWO_PI = 6283185307179586476925286766559005768394338798750 * 2 ** SCALE // 10 ** 48
PERIODS = 4096


def angle_parts(value, lowest_bits):
    parts = []
    for bit in lowest_bits:
        unit = 2 ** (SCALE + bit)
        n = (2 * value + unit) // (2 * unit)
        parts.append(float(n) * 2.0 ** bit)
        value -= n * unit
    return parts


COARSE = angle_parts(TWO_PI * PERIODS, (8, 1, -6, -13, -20, -27, -34))
FINE = angle_parts(TWO_PI, (-9, -21, -33))
ROUND = 1.5 * 2.0 ** 23


def build(nc, a, out):
    with ExitStack() as ctx:
        def sb(name, shape, dt=F32):
            return ctx.enter_context(nc.sbuf_tensor(name, shape, dt))

        def sem(name):
            return ctx.enter_context(nc.semaphore(name))

        xt = sb("xt", [P, M, D_MODEL])
        work = sb("work", [P, KFF * SEQ])
        xT_hi = sb("xT_hi", [P, KD, SEQ], F32R)
        xT_lo = sb("xT_lo", [P, KD, SEQ], F32R)
        pT_hi = sb("pT_hi", [P, PLE_PANELS, SEQ], F32R)
        pT_lo = sb("pT_lo", [P, PLE_PANELS, SEQ], F32R)
        raw = sb("raw", [P, RAW_SLOTS, PANEL])
        w_hi = sb("w_hi", [P, SPLIT_SLOTS, PANEL], F32R)
        w_lo = sb("w_lo", [P, SPLIT_SLOTS, PANEL], F32R)
        vec = sb("vec", [P, 2, D_MODEL])
        scratch = sb("scratch", [P, 6656])
        cosine = sb("cosine", [P, M, FREQS])
        sine = sb("sine", [P, M, FREQS])
        ident = sb("ident", [P, P])
        band = sb("band", [P, 2 * P])
        causal = sb("causal", [P, P])
        decay = sb("decay", [P, M, 2 * RET_HEADS])
        position = sb("position", [P, M], I32)
        position_f = sb("position_f", [P, M])
        sinks = sb("sinks", [P, ATT_HEADS])
        small = sb("small", [P, 96])

        proj = work[:, 0:M * IN_WIDTH].rearrange("p (m c) -> p m c", m=M)
        gated = work[:, :].rearrange("p (f t) -> p f t", t=SEQ)

        freq = scratch[:, 0:FREQS]
        angle = scratch[:, 320:640].rearrange("p (m f) -> p m f", m=M)
        coarse_k = scratch[:, 640:960].rearrange("p (m f) -> p m f", m=M)
        fine_k = scratch[:, 960:1280].rearrange("p (m f) -> p m f", m=M)
        p_tok = scratch[:, 0:M * PLE_DIM].rearrange("p (m c) -> p m c", m=M)
        rot_a = scratch[:, 2048:3072]
        rot_b = scratch[:, 3072:4096]
        k_twice = scratch[:, 4096:4608].rearrange("p (m k e d) -> p m k e d", m=M, k=ATT_KV, e=2)
        aqT = scratch[:, 0:2048].rearrange("p (c t) -> p c t", t=SEQ)
        akT = scratch[:, 6144:6656].rearrange("p (c t) -> p c t", t=SEQ)
        rqT = scratch[:, 2048:4096].rearrange("p (c t) -> p c t", t=SEQ)
        rkT = scratch[:, 4096:6144].rearrange("p (c t) -> p c t", t=SEQ)
        probs = [scratch[:, 2048 + 1024 * u:3072 + 1024 * u].rearrange("p (h k) -> p h k", h=4) for u in range(2)]
        probsT = [scratch[:, 4096 + 1024 * u:5120 + 1024 * u].rearrange("p (h k) -> p h k", h=4) for u in range(2)]
        scoresT = [proj[:, 0, 512 * h:512 * h + 384] for h in range(RET_HEADS)]
        attT = proj[:, :, AQ:AK].rearrange("p m (c t) -> p c m t", t=P)
        gate_sums = work[:, 4096:8192].rearrange("p (n c) -> p n c", n=4)
        ret_y = scratch[:, 0:2048].rearrange("p (m c) -> p m c", m=M)
        ret_sig = vec[:, 1, :].rearrange("p (m c) -> p m c", m=M)
        pool_rot_a, pool_rot_b = vec[:, 1, 0:1024], vec[:, 1, 1024:]
        square = scratch[:, 2048:4096]
        ple = scratch[:, 0:4096].rearrange("p (m c) -> p m c", m=M)
        tmp = [scratch[:, 4096:5120], scratch[:, 5120:6144]]
        conv_rows = scratch[:, 4096:4608].rearrange("p (k c) -> p k c", k=4)
        conv = scratch[:, 6144:6144 + 4 * 2 * KFF].rearrange("p (k c) -> p k c", k=4)
        bank_sums = small[:, 0:8].rearrange("p (m n) -> p m n", m=M)
        mean_neg = small[:, 48:50]
        squares = small[:, 50:52]
        rstd = small[:, 52:54]
        mean_off = small[:, 86:88]
        unused = small[:, 88:89]
        ret_moments = small[:, 0:16].rearrange("p (m h s) -> p m h s", m=M, h=RET_HEADS)
        ret_stats = small[:, 16:22]
        ret_rstd = small[:, 24:32].rearrange("p (m h) -> p m h", m=M)
        row_max = [small[:, 54 + 4 * u:58 + 4 * u] for u in range(2)]
        neg_max = [small[:, 62 + 4 * u:66 + 4 * u] for u in range(2)]
        sink_gap = [small[:, 70 + 4 * u:74 + 4 * u] for u in range(2)]
        row_sum = [small[:, 78 + 4 * u:82 + 4 * u] for u in range(2)]
        conv_group = small[:, 0:32].rearrange("p (k h c) -> p k h c", k=4, h=2)

        ps = ctx.enter_context(nc.psum_tensor("ps", [P, 8, BANK], F32))

        raw_arrived = [sem(f"raw_arrived{s}") for s in range(RAW_SLOTS)]
        hi_split = sem("hi_split")
        panels_split = sem("panels_split")
        panels_used = sem("panels_used")
        banks_made = sem("banks_made")
        x_loaded = [sem(f"x_loaded{h}") for h in range(2)]
        ident_loaded = sem("ident_loaded")
        consts_loaded = sem("consts_loaded")
        freq_loaded = sem("freq_loaded")
        p_loaded = sem("p_loaded")
        sinks_loaded = sem("sinks_loaded")
        ret_vec_loaded = sem("ret_vec_loaded")
        ln_vec_loaded = sem("ln_vec_loaded")
        ple_vec_loaded = sem("ple_vec_loaded")
        conv_loaded = sem("conv_loaded")
        stored = sem("stored")
        angles_reduced = sem("angles_reduced")
        tables_made = sem("tables_made")
        left_normed = sem("left_normed")
        right_normed = [sem(f"right_normed{m}") for m in range(M)]
        transposed = sem("transposed")
        xT_hi_done = sem("xT_hi_done")
        xT_lo_done = sem("xT_lo_done")
        proj_copied = sem("proj_copied")
        att_rotated = sem("att_rotated")
        ret_rotated = sem("ret_rotated")
        aqk_transposed = sem("aqk_transposed")
        aqk_copied = sem("aqk_copied")
        rqk_transposed = sem("rqk_transposed")
        rqk_copied = sem("rqk_copied")
        scores_done = sem("scores_done")
        max_done = sem("max_done")
        exp_done = sem("exp_done")
        probs_done = sem("probs_done")
        probsT_done = sem("probsT_done")
        probsT_copied = sem("probsT_copied")
        att_done = sem("att_done")
        att_copied = sem("att_copied")
        att_hi = sem("att_hi")
        att_lo = sem("att_lo")
        ret_scores_done = sem("ret_scores_done")
        ret_cross_copied = sem("ret_cross_copied")
        ret_scores_masked = sem("ret_scores_masked")
        ret_done = sem("ret_done")
        ret_copied = sem("ret_copied")
        ret_var = sem("ret_var")
        ret_std = sem("ret_std")
        ret_sigmoid = sem("ret_sigmoid")
        ret_silu = sem("ret_silu")
        ret_gains = sem("ret_gains")
        ret_normed = sem("ret_normed")
        ret_gated = [sem(f"ret_gated{pair}") for pair in range(2)]
        ret_transposed = sem("ret_transposed")
        ret_hi = sem("ret_hi")
        ret_lo = sem("ret_lo")
        sums_taken = sem("sums_taken")
        ln_mean = sem("ln_mean")
        ln_squares = sem("ln_squares")
        ln_var = sem("ln_var")
        ln_std = sem("ln_std")
        ln_ready = sem("ln_ready")
        ln_centred = sem("ln_centred")
        ple_copied = sem("ple_copied")
        conv_transposed = sem("conv_transposed")
        conv_copied = sem("conv_copied")
        conv_begun = sem("conv_begun")
        conv_group_set = sem("conv_group_set")
        gate_conv = sem("gate_conv")
        gate_sigmoid = sem("gate_sigmoid")
        up_taken = sem("up_taken")
        ple_sums = sem("ple_sums")
        ple_sigmoid = sem("ple_sigmoid")
        ple_used = sem("ple_used")
        g_hi = sem("g_hi")
        g_split = sem("g_split")
        waits_met = sem("waits_met")
        act_step = sem("act_step")
        dve_step = sem("dve_step")
        pool_step = sem("pool_step")

        def rotate(tt, link, heads, table, m, rot_a, rot_b):
            n, half = heads.shape[1], heads.shape[3]
            x1, x2 = heads[:, :, 0, :], heads[:, :, 1, :]
            cos = cosine[:, m, table:table + half].unsqueeze(1).to_broadcast([P, n, half])
            sin = sine[:, m, table:table + half].unsqueeze(1).to_broadcast([P, n, half])
            x1_sin = rot_a[:, 0:n * half].rearrange("p (h f) -> p h f", h=n)
            x2_sin = rot_b[:, 0:n * half].rearrange("p (h f) -> p h f", h=n)
            tt(x1_sin, x1, sin, ALU.mult)
            link(tt(x2_sin, x2, sin, ALU.mult))
            tt(x1, x1, cos, ALU.mult)
            link(tt(x2, x2, cos, ALU.mult))
            tt(x1, x1, x2_sin, ALU.subtract)
            link(tt(x2, x2, x1_sin, ALU.add))

        def rotate_attention(eng, tt, copy, link, l, m, rot_a, rot_b):
            eng.wait_ge(proj_copied, layered(l, COPIES, M * (1 + AQ_MADE // HALF_PANELS) + 1))
            rotate(tt, link, proj[:, m, AQ:AV].rearrange("p (h e f) -> p h e f", e=2, f=ATT_DIM // 2),
                   RET_DIM // 2, m, rot_a, rot_b)
            stand_alone(eng)
            for kv in range(ATT_KV):
                k = proj[:, m, AK + kv * ATT_DIM:AK + (kv + 1) * ATT_DIM]
                last = copy(k_twice[:, m, kv, :, :], k.unsqueeze(1).to_broadcast([P, 2, ATT_DIM]))
            link(last)
            eng.sem_inc(att_rotated, 1)

        def ret_gate(eng, tt, link, l, pair):
            eng.wait_ge(ret_gains, layered(l, 1, 1))
            cols = slice(512 * pair, 512 * pair + 512)
            y = ret_y[:, :, cols]
            link(tt(y, y, proj[:, :, RG:AQ][:, :, cols], ALU.mult))
            tt(y, y, ret_sig[:, :, cols], ALU.add).then_inc(ret_gated[pair], 1)

        def stand_alone(eng):
            eng.sem_inc(waits_met, 1)

        block = ctx.enter_context(nc.Block())

        @block.sync
        def _(sp):
            def load(l, at, i, step, src, shape):
                s = at % RAW_SLOTS
                k, w = shape
                sp.wait_ge(panels_split, layered(l, PANELS, at + 1) + i * step)
                stand_alone(sp)
                sp.dma_start(raw[:, s, :].rearrange("p (k w) -> p k w", k=k),
                             src.rearrange("(k p) w -> p k w", p=P)).then_inc(raw_arrived[s], 16)

            sp.dma_start(freq, a["c_freq"].to_broadcast([P, FREQS])).then_inc(freq_loaded, 16)
            for m in range(M):
                sp.dma_start(position[:, m:m + 1],
                             a["positions"][0, m * P:(m + 1) * P].rearrange("(p o) -> p o", o=1)).then_inc(freq_loaded, 16)
            sp.dma_start(ident[:, :], a["c_ident"]).then_inc(ident_loaded, 16)
            for half, loaded in enumerate(x_loaded):
                cols = slice(half * 1024, (half + 1) * 1024)
                sp.dma_start(xt[:, :, cols], a["x"][0, :, cols].rearrange("(m p) c -> p m c", p=P)).then_inc(loaded, 16)
            with sp.Fori(0, DEPTH) as l:
                for n in range(KV_PANELS):
                    load(l, KV_AT + n, 0, 0, a["w_in"][l, n * 1024:(n + 1) * 1024, AK:IN_WIDTH], (8, 256))
                for q, col in enumerate(HALVES):
                    for j in range(HALF_PANELS):
                        load(l, IN_AT + HALF_PANELS * q + j, 0, 0,
                             a["w_in"][l, j * 512:(j + 1) * 512, col:col + 512], (4, 512))
                for n in range(8):
                    row, col = RET_WIDTH + (n % 4) * 256, (n // 4) * 1024
                    load(l, OUT_AT + n, 0, 0, a["w_out"][l, row:row + 256, col:col + 1024], (2, 1024))
                for n in range(8, OUT_PANELS):
                    load(l, OUT_AT + n, 0, 0, a["w_out"][l, (n - 8) * P:(n - 7) * P, :], (1, D_MODEL))
                for n in range(PLE_PANELS):
                    load(l, PLE_AT + n, 0, 0, a["w_ple_proj"][l, n * P:(n + 1) * P, :], (1, D_MODEL))
                for n in range(GATE_PANELS):
                    load(l, GATE_AT + n, 0, 0, a["w_ple_gate"][l, n * P:(n + 1) * P, :], (1, D_MODEL))
                with sp.Fori(0, FF_GROUPS) as i:
                    for j in range(UP_BODY):
                        load(l, UP_AT + j, i, UP_BODY,
                             a["w_ffn_up"][l, (j % 4) * 512:(j % 4 + 1) * 512,
                                           bass.ds(i * 512 + (j // 4) * D_FF, 512)], (4, 512))
                with sp.Fori(0, KFF // 4) as i:
                    for j in range(4):
                        load(l, DOWN_AT + j, i, 4, a["w_ffn_down"][l, bass.ds(i * 512 + j * P, P), :], (1, D_MODEL))
            for half in range(2):
                for m in range(M):
                    cols = slice(half * 1024, half * 1024 + 1024)
                    if half == 0:
                        sp.wait_ge(left_normed, M * 2 * DEPTH + m + 1)
                    else:
                        sp.wait_ge(right_normed[m], 2 * DEPTH + 1)
                    sp.dma_start(out[0, m * P:(m + 1) * P, cols], xt[:, m, cols]).then_inc(stored, 16)
            sp.wait_ge(stored, 16 * 2 * M)

        @block.gpsimd
        def _(pool):
            link = Chain(pool, pool_step)
            for dst, src in ((band, "c_band"), (causal, "c_causal")):
                pool.dma_start(dst[:, :], a[src]).then_inc(consts_loaded, 16)
            pool.dma_start(decay[:, :, :], a["c_decay"]).then_inc(consts_loaded, 16)

            def everywhere(dst, row, signal):
                pool.dma_start(dst, row.to_broadcast([P, row.shape[1]])).then_inc(signal, 16)

            def normalise_second(l, norm):
                pool.wait_ge(ln_vec_loaded, layered(l, 64, 32 * (1 + norm)))
                pool.wait_ge(ln_centred, layered(l, 2 * M, norm * M + 1))
                x = xt[:, 0, 1024:]
                link(nc.gpsimd.tensor_tensor(x, x, vec[:, 1, 1024:], ALU.mult))
                nc.gpsimd.tensor_tensor(x, x, vec[:, 0, 1024:], ALU.add).then_inc(right_normed[0], 1)

            pool.sem_inc(right_normed[0], 1)
            pool.wait_ge(tables_made, 1)
            pool.wait_ge(consts_loaded, 48)
            with link.loop(DEPTH, POOL_LINKS) as l:
                pool.wait_ge(left_normed, layered(l, 2 * M, M))
                for normed in right_normed:
                    pool.wait_ge(normed, layered(l, 2, 1))
                stand_alone(pool)
                pool.dma_start(p_tok, a["p"][l, 0].rearrange("(m p) c -> p m c", p=P)).then_inc(p_loaded, 16)
                everywhere(sinks[:, :], a["attn_sinks"][bass.ds(l, 1), :], sinks_loaded)
                everywhere(vec[:, 0, 0:RET_WIDTH], a["ret_norm_g"][bass.ds(l, 1), :], ret_vec_loaded)
                everywhere(vec[:, 0, RET_WIDTH:], a["ret_norm_b"][bass.ds(l, 1), :], ret_vec_loaded)

                rotate_attention(pool, nc.gpsimd.tensor_tensor, nc.gpsimd.tensor_copy, link, l, 1,
                                 pool_rot_a, pool_rot_b)

                for n, first in enumerate((RQ, RK)):
                    pool.wait_ge(proj_copied, layered(l, COPIES, M * (1 + (RQ_MADE, RK_MADE)[n] // HALF_PANELS) + 1))
                    for m in range(M):
                        heads = proj[:, m, first:first + RET_WIDTH]
                        rotate(nc.gpsimd.tensor_tensor, link,
                               heads.rearrange("p (h e f) -> p h e f", e=2, f=RET_DIM // 2), 0, m, pool_rot_a, pool_rot_b)
                        heads = heads.rearrange("p (h c) -> p h c", c=RET_DIM)
                        factors = decay[:, m, RET_HEADS * n:RET_HEADS * (n + 1)].unsqueeze(2)
                        link(nc.gpsimd.tensor_tensor(
                            heads, heads, factors.to_broadcast([P, RET_HEADS, RET_DIM]), ALU.mult))
                    pool.sem_inc(ret_rotated, 1)

                pool.wait_ge(ret_silu, layered(l, 1, 1))
                pool.wait_ge(ret_vec_loaded, layered(l, 32, 32))
                silu = proj[:, :, RG:AQ]
                for dst, v in ((ret_sig, vec[:, 0, RET_WIDTH:]), (silu, vec[:, 0, 0:RET_WIDTH])):
                    link(nc.gpsimd.tensor_tensor(dst, silu, v.unsqueeze(1).to_broadcast([P, M, RET_WIDTH]), ALU.mult))
                pool.sem_inc(ret_gains, 1)
                pool.wait_ge(ret_normed, layered(l, 1, 1))
                ret_gate(pool, nc.gpsimd.tensor_tensor, link, l, 0)

                for gated_pair in ret_gated:
                    pool.wait_ge(gated_pair, layered(l, 1, 1))
                stand_alone(pool)
                everywhere(vec[:, 1, :], a["ln1_g"][bass.ds(l, 1), :], ln_vec_loaded)
                everywhere(vec[:, 0, :], a["ln1_b"][bass.ds(l, 1), :], ln_vec_loaded)
                for k in range(3):
                    pool.dma_start(conv_rows[0:2 * KFF, k, :],
                                   a["ffn_conv_w"][l, k].rearrange("(c f) -> c f", f=P)).then_inc(conv_loaded, 16)
                pool.dma_start(conv_rows[0:2 * KFF, 3, :],
                               a["ffn_conv_b"][l].rearrange("(c f) -> c f", f=P)).then_inc(conv_loaded, 16)
                normalise_second(l, 0)
                pool.wait_ge(left_normed, layered(l, 2 * M, 2 * M))
                for normed in right_normed:
                    pool.wait_ge(normed, layered(l, 2, 2))
                stand_alone(pool)
                everywhere(vec[:, 0, :], a["b_ple_gate"][bass.ds(l, 1), :], ple_vec_loaded)
                everywhere(vec[:, 1, :], a["ln2_g"][bass.ds(l, 1), :], ln_vec_loaded)
                pool.wait_ge(ple_sums, layered(l, 4, 4))
                stand_alone(pool)
                everywhere(vec[:, 0, :], a["ln2_b"][bass.ds(l, 1), :], ln_vec_loaded)
                normalise_second(l, 1)

        @block.scalar
        def _(act):
            link = Chain(act, act_step)

            def split(l, at, i=0, step=0):
                act.wait_ge(raw_arrived[at % RAW_SLOTS],
                            (layered(l, PANELS // RAW_SLOTS, at // RAW_SLOTS + 1) + i * (step // RAW_SLOTS)) * 16)
                act.wait_ge(panels_used, layered(l, PANELS, at + 1) + i * step)
                nc.scalar.copy(w_hi[:, at % SPLIT_SLOTS, :], raw[:, at % RAW_SLOTS, :]).then_inc(hi_split, 1)

            def used(l, n):
                return layered(l, PANELS, n + SPLIT_SLOTS)

            def take_transposed(l, norm):
                for b in range(XT_BANKS):
                    act.wait_ge(transposed, layered(l, T_BANKS, norm * (XT_BANKS + 1) + b + 1))
                    nc.scalar.copy(xT_hi[:, 2 * b:2 * b + 2, :].rearrange("p k t -> p (k t)"),
                                   ps[:, XT_PSUM[norm][b], :]).then_inc(xT_hi_done, 1)

            def norm_squares(l, norm, m):
                act.wait_ge(ln_mean, layered(l, 2 * M, norm * M + m + 1))
                nc.scalar.activation(square, xt[:, m, :], ACT.Square, bias=mean_neg[:, m:m + 1],
                                     accum_out=squares[:, m:m + 1]).then_inc(ln_squares, 1)

            def norm_root(l, norm, m):
                act.wait_ge(ln_var, layered(l, 2 * M, norm * M + m + 1))
                nc.scalar.activation(rstd[:, m:m + 1], rstd[:, m:m + 1], ACT.Sqrt).then_inc(ln_std, 1)

            def norm_centre(l, norm):
                for m in range(M):
                    act.wait_ge(ln_ready, layered(l, 2 * M, norm * M + m + 1))
                    nc.scalar.activation(xt[:, m, 1024:], xt[:, m, 1024:], ACT.Identity,
                                         bias=mean_off[:, m:m + 1], scale=rstd[:, m:m + 1]).then_inc(ln_centred, 1)

            act.sem_inc(proj_copied, 1)
            act.wait_ge(angles_reduced, 2)
            nc.scalar.activation(sine[:, :, :], angle, ACT.Sin)
            nc.scalar.activation(cosine[:, :, :], fine_k, ACT.Sin).then_inc(tables_made, 1)

            with link.loop(DEPTH, 0) as l:
                split(l, KV_AT)
                take_transposed(l, 0)
                split(l, KV_AT + 1)
                split(l, IN_AT)
                act.wait_ge(transposed, layered(l, T_BANKS, XT_BANKS + 1))
                nc.scalar.copy(pT_hi[:, :, :].rearrange("p k t -> p (k t)"), ps[:, P_PSUM, :]).then_inc(xT_hi_done, 1)
                act.wait_ge(panels_used, used(l, IN_AT))
                for m in range(M):
                    nc.scalar.copy(proj[:, m, AK:IN_WIDTH], ps[:, m, 0:256]).then_inc(proj_copied, 1)

                def take_half(q):
                    act.wait_ge(panels_used, used(l, IN_AT + HALF_PANELS * (q + 1)))
                    for m in range(M):
                        nc.scalar.copy(proj[:, m, HALVES[q]:HALVES[q] + 512],
                                       ps[:, 2 - 2 * (q % 2) + m, :]).then_inc(proj_copied, 1)

                def take_aqk(n):
                    act.wait_ge(aqk_transposed, layered(l, AQK_BANKS, n + 1))
                    dst = akT if n == 0 else aqT[:, 2 * n - 2:2 * n]
                    nc.scalar.copy(dst.rearrange("p c t -> p (c t)"), ps[:, AQK_PSUM[n], :]).then_inc(aqk_copied, 1)

                def exponentials(n):
                    u, keys = n % 2, P * (1 + n // 4)
                    act.wait_ge(max_done, layered(l, UNITS, n + 1))
                    for h in range(4):
                        nc.scalar.activation(probs[u][:, h, 0:keys], probs[u][:, h, 0:keys], ACT.Exp,
                                             bias=neg_max[u][:, h:h + 1], accum_out=row_sum[u][:, h:h + 1])
                    nc.scalar.activation(sink_gap[u], sink_gap[u], ACT.Exp).then_inc(exp_done, 1)

                def take_probsT(n):
                    u, keys = n % 2, P * (1 + n // 4)
                    act.wait_ge(probsT_done, layered(l, UNITS, n + 1))
                    for b in range(2):
                        nc.scalar.copy(
                            probsT[u][:, 2 * b:2 * b + 2, 0:keys],
                            ps[:, 6 + b, :].rearrange("p (h k) -> p h k", h=2)[:, :, 0:keys]).then_inc(probsT_copied, 1)

                def take_attention(n):
                    m, quad = n // 4, n % 4
                    act.wait_ge(att_done, layered(l, UNITS, n + 1))
                    nc.scalar.copy(attT[:, 2 * quad:2 * quad + 2, m, :],
                                   ps[:, 6, 0:256].rearrange("p (c t) -> p c t", c=2)).then_inc(att_copied, 1)

                def take_rqk(n):
                    act.wait_ge(rqk_transposed, layered(l, 8, RQK_ORDER.index(n) + 1))
                    dst = rqT[:, 2 * n:2 * n + 2] if n < 4 else rkT[:, 2 * n - 8:2 * n - 6]
                    nc.scalar.copy(dst.rearrange("p c t -> p (c t)"), ps[:, 4 + n % 2, :]).then_inc(rqk_copied, 1)

                def take_cross_scores(h):
                    act.wait_ge(ret_scores_done, layered(l, RET_HEADS, h + 1))
                    nc.scalar.copy(scoresT[h][:, 256:384], ps[:, 6 + h % 2, 256:384]).then_inc(ret_cross_copied, 1)

                def take_retention(h):
                    act.wait_ge(ret_done, layered(l, RET_HEADS, h + 1))
                    nc.scalar.copy(ret_y[:, :, h * 256:(h + 1) * 256],
                                   ps[:, 4 + h, :].rearrange("p (m c) -> p m c", m=M)).then_inc(ret_copied, 1)

                def ret_root(pair):
                    act.wait_ge(ret_var, layered(l, 2, pair + 1))
                    r = ret_rstd[:, :, 2 * pair:2 * pair + 2]
                    nc.scalar.activation(r, r, ACT.Sqrt).then_inc(ret_std, 1)

                def take_ret_transposed(pair):
                    for b in (2 * pair, 2 * pair + 1):
                        act.wait_ge(ret_transposed, layered(l, 4, b + 1))
                        nc.scalar.copy(xT_hi[:, 2 * b:2 * b + 2, :].rearrange("p k t -> p (k t)"),
                                       ps[:, RET_PSUM[b], :]).then_inc(ret_hi, 1)

                def split_attention(j):
                    act.wait_ge(panels_used, used(l, OUT_AT - (j < 2)))
                    act.wait_ge(att_copied, layered(l, UNITS, UNITS))
                    nc.scalar.copy(xT_hi[:, 8 + 2 * j:10 + 2 * j, :].rearrange("p c (m t) -> p c m t", m=M),
                                   attT[:, 2 * j:2 * j + 2, :, :]).then_inc(att_hi, 1)

                for s in range(STEPS):
                    if s == RV_MADE + 4:
                        take_ret_transposed(1)
                    if s == RV_MADE:
                        take_half(s // HALF_PANELS - 1)
                    split(l, IN_AT + s + 1)
                    if s and s % HALF_PANELS == 0 and s < RV_MADE:
                        take_half(s // HALF_PANELS - 1)
                    for n in AQK_TRANSPOSE.get(s - 1, ()):
                        take_aqk(n)
                    if (n := unit(s, TAKE_P)) is not None:
                        take_probsT(n)
                    if (n := unit(s, TAKE_O)) is not None:
                        take_attention(n)
                    if (n := unit(s, EXPONENTIALS)) is not None:
                        exponentials(n)
                    for n in RQK_TRANSPOSE.get(s - 1, ()):
                        take_rqk(n)
                    if 0 <= s - 1 - RET_SCORES < RET_HEADS:
                        take_cross_scores(s - 1 - RET_SCORES)
                    if s == SILU:
                        act.wait_ge(ret_rotated, layered(l, 2, 2))
                        act.wait_ge(proj_copied, layered(l, COPIES, M * (1 + RG_MADE // HALF_PANELS) + 1))
                        nc.scalar.activation(ret_sig, proj[:, :, RG:AQ], ACT.Sigmoid).then_inc(ret_sigmoid, 1)
                    for pair in range(2):
                        if s == RET_PV[pair] + 1:
                            take_retention(2 * pair)
                            take_retention(2 * pair + 1)
                        if s == RET_PV[pair] + 2:
                            ret_root(pair)
                    if s in (RV_MADE - 1, RV_MADE):
                        for j in (2 * (s - RV_MADE + 1), 2 * (s - RV_MADE + 1) + 1):
                            split_attention(j)
                    if s == RV_MADE + 2:
                        take_ret_transposed(0)

                for n in range(8, OUT_PANELS):
                    split(l, OUT_AT + n + 1)
                norm_squares(l, 0, 0)
                split(l, PLE_AT + 1)
                norm_root(l, 0, 0)
                act.wait_ge(conv_transposed, layered(l, 1, 1))
                nc.scalar.copy(conv, ps[:, 0, 0:4 * 2 * KFF].rearrange("p (k c) -> p k c", k=4)).then_inc(conv_copied, 1)
                norm_squares(l, 0, 1)
                split(l, GATE_AT)
                norm_root(l, 0, 1)
                norm_centre(l, 0)
                act.wait_ge(panels_used, used(l, GATE_AT))
                for b in PLE_BANKS:
                    nc.scalar.copy(ple[:, b // 4, (b % 4) * BANK:(b % 4 + 1) * BANK], ps[:, b, :]).then_inc(ple_copied, 1)
                take_transposed(l, 1)

                for n in range(GATE_PANELS):
                    split(l, GATE_AT + n + 1)

                def begin_conv(half, p, i):
                    if p < 2:
                        act.wait_ge(panels_used, used(l, UP_AT + 4 * half + 4) + i * UP_BODY)
                        act.wait_ge(conv_group_set, layered(l, TAPS, half + 1) + i * 2)
                        for c in (2 * p, 2 * p + 1):
                            if half == 0:
                                dst = work[:, bass.ds(i * (FF_GROUP * SEQ) + c * SEQ, SEQ)]
                            else:
                                dst = tmp[1][:, c * SEQ:(c + 1) * SEQ]
                            last = nc.scalar.activation(
                                dst, ps[:, 2 * half + p, (c % 2) * SEQ:(c % 2 + 1) * SEQ], ACT.Identity,
                                bias=conv_group[:, 3, half, c:c + 1], scale=conv_group[:, 2, half, c:c + 1])
                        last.then_inc(conv_begun, 1)
                    elif p == 2 and half == 0:
                        act.wait_ge(gate_conv, layered(l, FF_GROUPS, 2) + i)
                        stand_alone(act)
                        nc.scalar.activation(tmp[0], work[:, bass.ds(i * (FF_GROUP * SEQ), FF_GROUP * SEQ)],
                                             ACT.Sigmoid).then_inc(gate_sigmoid, 1)

                split(l, UP_AT + 1)
                for n in range(4):
                    act.wait_ge(ple_sums, layered(l, 4, n + 1))
                    nc.scalar.activation(gate_sums[:, n, :], gate_sums[:, n, :], ACT.Sigmoid).then_inc(ple_sigmoid, 1)
                    if n:
                        split(l, UP_AT + n + 1)
                with act.Fori(0, FF_GROUPS - 1) as i:
                    for j in range(UP_BODY):
                        split(l, UP_AT + 4 + j + 1, i, UP_BODY)
                        begin_conv(j // 4, j % 4, i)

                def down_step(j, i):
                    split(l, DOWN_AT + j, i, 4)
                    act.wait_ge(panels_used, used(l, DOWN_AT + j - 3) + i * 4)
                    nc.scalar.copy(xT_hi[:, j % 4, :], work[:, bass.ds(i * (4 * SEQ) + j * SEQ, SEQ)]).then_inc(g_hi, 1)

                for j in range(4):
                    if j < 3:
                        split(l, DOWN_AT - 4 + j + 1)
                    else:
                        down_step(0, 0)
                    begin_conv(0, j, FF_GROUPS - 1)

                for j in range(4):
                    if j == 0:
                        begin_conv(1, 0, FF_GROUPS - 1)
                        begin_conv(1, 1, FF_GROUPS - 1)
                    down_step(j + 1, 0)
                with act.Fori(1, KFF // 4 - 1) as i:
                    for j in range(4):
                        down_step(j + 1, i)
                for j in range(3):
                    down_step(j + 1, KFF // 4 - 1)
                nc.scalar.activation(unused, ident[:, 0:1], ACT.Sqrt)
                for m in range(M):
                    norm_squares(l, 1, m)
                    norm_root(l, 1, m)
                norm_centre(l, 1)

        @block.vector
        def _(dve):
            link = Chain(dve, dve_step)
            tt, ts, stt = nc.vector.tensor_tensor, nc.vector.tensor_scalar, nc.vector.scalar_tensor_tensor

            def used(l, n):
                return layered(l, PANELS, n + SPLIT_SLOTS)

            def split(l, at, i=0, step=0):
                dve.wait_ge(hi_split, layered(l, PANELS, at + 1) + i * step)
                tt(w_lo[:, at % SPLIT_SLOTS, :], raw[:, at % RAW_SLOTS, :],
                   w_hi[:, at % SPLIT_SLOTS, :].bitcast(F32), ALU.subtract).then_inc(panels_split, 1)

            def take_transposed(l, norm):
                for b in range(XT_BANKS):
                    dve.wait_ge(xT_hi_done, layered(l, T_BANKS, norm * (XT_BANKS + 1) + b + 1))
                    tt(xT_lo[:, 2 * b:2 * b + 2, :].rearrange("p k t -> p (k t)"), ps[:, XT_PSUM[norm][b], :],
                       xT_hi[:, 2 * b:2 * b + 2, :].rearrange("p k t -> p (k t)").bitcast(F32),
                       ALU.subtract).then_inc(xT_lo_done, 1)

            def bank_made(l, products, stage, b):
                if b < 7:
                    dve.wait_ge(banks_made, layered(l, BANKS_MADE, 7 * stage + b + 1))
                else:
                    dve.wait_ge(panels_used, used(l, products))

            def add_and_norm(l, products, stage, factor, norm, splits=()):
                for b in range(8):
                    if b == 2 and splits:
                        split(l, splits[0])
                    bank_made(l, products, stage, b)
                    m, n = b // 4, b % 4
                    part = xt[:, m, n * BANK:(n + 1) * BANK]
                    stt(part, part, factor, ps[:, b, :], ALU.mult, ALU.add,
                        accum_out=bank_sums[:, m, n:n + 1]).then_inc(sums_taken, 1)
                    if n == 3:
                        dve.wait_ge(sums_taken, layered(l, 16, 8 * norm + b + 1))
                        link(nc.vector.reduce_sum(mean_neg[:, m:m + 1], bank_sums[:, m, :], AX_X))
                        ts(mean_neg[:, m:m + 1], mean_neg[:, m:m + 1], -1.0 / D_MODEL, None,
                           ALU.mult).then_inc(ln_mean, 1)

                def variance(m):
                    dve.wait_ge(ln_squares, layered(l, 2 * M, norm * M + m + 1))
                    ts(rstd[:, m:m + 1], squares[:, m:m + 1], 1.0 / D_MODEL, LN_EPS, ALU.mult, ALU.add).then_inc(ln_var, 1)

                variance(0)
                if splits:
                    split(l, splits[1])
                dve.wait_ge(ln_vec_loaded, layered(l, 64, 32 * (1 + norm)))
                for m in range(M):
                    if m == 1:
                        variance(1)
                    dve.wait_ge(ln_std, layered(l, 2 * M, norm * M + m + 1))
                    link(nc.vector.reciprocal(rstd[:, m:m + 1], rstd[:, m:m + 1]))
                    tt(mean_off[:, m:m + 1], mean_neg[:, m:m + 1], rstd[:, m:m + 1], ALU.mult).then_inc(ln_ready, 1)
                    x = xt[:, m, 0:1024]
                    link(stt(x, x, mean_neg[:, m:m + 1], vec[:, 1, 0:1024], ALU.add, ALU.mult))
                    stt(x, x, rstd[:, m:m + 1], vec[:, 0, 0:1024], ALU.mult, ALU.add).then_inc(left_normed, 1)
                x = xt[:, 1, 1024:]
                dve.wait_ge(ln_centred, layered(l, 2 * M, norm * M + M))
                link(tt(x, x, vec[:, 1, 1024:], ALU.mult))
                tt(x, x, vec[:, 0, 1024:], ALU.add).then_inc(right_normed[1], 1)

            dve.sem_inc(panels_split, RAW_SLOTS)
            dve.sem_inc(gate_conv, 1)
            dve.sem_inc(up_taken, 1)
            dve.sem_inc(left_normed, M)
            dve.sem_inc(right_normed[1], 1)

            dve.wait_ge(freq_loaded, 16 * (M + 1))
            link(nc.vector.tensor_copy(position_f[:, :], position[:, :]))
            for m in range(M):
                last = ts(angle[:, m, :], freq, position_f[:, m:m + 1], None, ALU.mult)
            link(last)

            def turns(dst, src, turn):
                link(ts(dst, src, 1.0 / turn, ROUND, ALU.mult, ALU.add))
                link(ts(dst, dst, ROUND, None, ALU.subtract))

            def less(k, part):
                link(stt(angle, k, -part, angle, ALU.mult, ALU.add))

            turns(coarse_k, angle, 2.0 * np.pi * PERIODS)
            for part in COARSE[0:3]:
                less(coarse_k, part)
            link(stt(fine_k, coarse_k, -COARSE[3], angle, ALU.mult, ALU.add))
            turns(fine_k, fine_k, 2.0 * np.pi)
            for k, part in ((fine_k, FINE[0]), (coarse_k, COARSE[3]), (fine_k, FINE[1]), (coarse_k, COARSE[4]),
                            (fine_k, FINE[2]), (coarse_k, COARSE[5]), (coarse_k, COARSE[6])):
                less(k, part)
            pi = float(np.nextafter(np.float32(np.pi), np.float32(0)))
            link(ts(angle, angle, pi, -pi, ALU.min, ALU.max))
            link(stt(fine_k, angle, -1.0, angle, ALU.mult, ALU.max))
            ts(fine_k, fine_k, -1.0, float(np.pi / 2), ALU.mult, ALU.add).then_inc(angles_reduced, 2)

            with link.loop(DEPTH, LINKS) as l:
                split(l, KV_AT)
                take_transposed(l, 0)
                split(l, KV_AT + 1)
                split(l, IN_AT)
                dve.wait_ge(xT_hi_done, layered(l, T_BANKS, XT_BANKS + 1))
                tt(pT_lo[:, :, :].rearrange("p k t -> p (k t)"), ps[:, P_PSUM, :],
                   pT_hi[:, :, :].rearrange("p k t -> p (k t)").bitcast(F32), ALU.subtract).then_inc(xT_lo_done, 1)

                def maxima(n):
                    u, quad, keys = n % 2, n % 4, P * (1 + n // 4)
                    mask = (band[:, P:] if n < 4 else band[:, :]).unsqueeze(1).to_broadcast([P, 2, keys])
                    dve.wait_ge(scores_done, layered(l, UNITS, n + 1))
                    if n >= 2:
                        dve.wait_ge(probsT_done, layered(l, UNITS, n - 1))
                    for e in range(2):
                        scores = ps[:, 4 + e, :].rearrange("p (c k) -> p c k", c=2)[:, :, 0:keys]
                        last = stt(probs[u].rearrange("p (c e) k -> p e c k", e=2)[:, e, :, 0:keys], scores,
                                   ATT_DIM ** -0.5, mask, ALU.mult, ALU.add)
                    link(last)
                    sink = sinks[:, 4 * quad:4 * quad + 4]
                    link(nc.vector.reduce_max(row_max[u], probs[u][:, :, 0:keys], AX_X))
                    link(tt(row_max[u], row_max[u], sink, ALU.max))
                    ts(neg_max[u], row_max[u], -1.0, None, ALU.mult)
                    tt(sink_gap[u], sink, row_max[u], ALU.subtract).then_inc(max_done, 1)

                def normalise(n):
                    u, keys = n % 2, P * (1 + n // 4)
                    dve.wait_ge(exp_done, layered(l, UNITS, n + 1))
                    link(tt(row_sum[u], row_sum[u], sink_gap[u], ALU.add))
                    link(nc.vector.reciprocal(row_sum[u], row_sum[u]))
                    p = probs[u][:, :, 0:keys]
                    tt(p, p, row_sum[u].unsqueeze(2).to_broadcast([P, 4, keys]), ALU.mult).then_inc(probs_done, 1)

                def mask_scores(h):
                    dve.wait_ge(ret_cross_copied, layered(l, RET_HEADS, h + 1))
                    tt(scoresT[h][:, 0:256].rearrange("p (b t) -> p b t", b=2),
                       ps[:, 6 + h % 2, 0:256].rearrange("p (b t) -> p b t", b=2),
                       causal[:, :].unsqueeze(1).to_broadcast([P, 2, P]), ALU.mult).then_inc(ret_scores_masked, 1)

                def ret_statistics(pair):
                    for h in (2 * pair, 2 * pair + 1):
                        dve.wait_ge(ret_copied, layered(l, RET_HEADS, h + 1))
                        for m in range(M):
                            link(nc.vector.bn_stats(ret_stats, ret_y[:, m, h * RET_DIM:(h + 1) * RET_DIM]))
                            stand_alone(dve)
                            link(nc.vector.bn_aggr(ret_moments[:, m, h, :], ret_stats))
                    heads = slice(2 * pair, 2 * pair + 2)
                    ts(ret_rstd[:, :, heads], ret_moments[:, :, heads, 1], GN_EPS, None, ALU.add).then_inc(ret_var, 1)

                def ret_normalise(pair):
                    dve.wait_ge(ret_std, layered(l, 2, pair + 1))
                    r = ret_rstd[:, :, 2 * pair:2 * pair + 2]
                    link(nc.vector.reciprocal(r, r))
                    for m in range(M):
                        for h in (2 * pair, 2 * pair + 1):
                            y = ret_y[:, m, h * RET_DIM:(h + 1) * RET_DIM]
                            last = ts(y, y, ret_moments[:, m, h, 0:1], ret_rstd[:, m, h:h + 1], ALU.subtract, ALU.mult)
                    link(last)

                def take_ret_transposed(pair):
                    for b in (2 * pair, 2 * pair + 1):
                        dve.wait_ge(ret_hi, layered(l, 4, b + 1))
                        tt(xT_lo[:, 2 * b:2 * b + 2, :].rearrange("p k t -> p (k t)"), ps[:, RET_PSUM[b], :],
                           xT_hi[:, 2 * b:2 * b + 2, :].rearrange("p k t -> p (k t)").bitcast(F32),
                           ALU.subtract).then_inc(ret_lo, 1)

                def split_attention(j):
                    dve.wait_ge(att_hi, layered(l, 4, j + 1))
                    part = xT_hi[:, 8 + 2 * j:10 + 2 * j, :].rearrange("p c (m t) -> p c m t", m=M)
                    tt(xT_lo[:, 8 + 2 * j:10 + 2 * j, :].rearrange("p c (m t) -> p c m t", m=M),
                       attT[:, 2 * j:2 * j + 2, :, :], part.bitcast(F32), ALU.subtract).then_inc(att_lo, 1)

                dve.wait_ge(tables_made, 1)
                dve.wait_ge(consts_loaded, 48)
                dve.wait_ge(sinks_loaded, layered(l, 16, 16))
                for s in range(STEPS):
                    if s == RV_MADE + 4:
                        take_ret_transposed(1)
                    split(l, IN_AT + s + 1)
                    if s == AQ_MADE:
                        rotate_attention(dve, tt, nc.vector.tensor_copy, link, l, 0, rot_a, rot_b)
                    if (n := unit(s, NORMALISE)) is not None:
                        normalise(n)
                    if (n := unit(s, MAXIMA)) is not None:
                        maxima(n)
                    if 0 <= s - 1 - RET_SCORES < RET_HEADS:
                        mask_scores(s - 1 - RET_SCORES)
                    if s == SILU + 1:
                        dve.wait_ge(ret_sigmoid, layered(l, 1, 1))
                        g = proj[:, :, RG:AQ]
                        tt(g, g, ret_sig, ALU.mult).then_inc(ret_silu, 1)
                    for pair in range(2):
                        if s == RET_PV[pair] + 1:
                            ret_statistics(pair)
                        if s == RET_PV[pair] + 2:
                            ret_normalise(pair)
                            if pair == 0:
                                dve.sem_inc(ret_normed, 1)
                            else:
                                ret_gate(dve, tt, link, l, 1)
                    if s in (RV_MADE - 1, RV_MADE):
                        for j in (2 * (s - RV_MADE + 1), 2 * (s - RV_MADE + 1) + 1):
                            split_attention(j)
                    if s == RV_MADE + 2:
                        take_ret_transposed(0)

                for n in range(8, OUT_PANELS - 1):
                    split(l, OUT_AT + n + 1)
                add_and_norm(l, PLE_AT, 0, ALPHA, 0, (PLE_AT, PLE_AT + 1))
                split(l, GATE_AT)
                take_transposed(l, 1)

                for n in range(GATE_PANELS):
                    split(l, GATE_AT + n + 1)

                def set_taps(half, i):
                    link(nc.vector.tensor_copy(conv_group[:, :, half, :],
                                               conv[:, :, bass.ds(i * FF_GROUP + half * KFF, FF_GROUP)]))
                    dve.sem_inc(conv_group_set, 1)

                def convolve(half, p, i):
                    group = work[:, bass.ds(i * (FF_GROUP * SEQ), FF_GROUP * SEQ)]
                    if p < 2:
                        dve.wait_ge(conv_begun, layered(l, 4 * FF_GROUPS, 2 * half + p + 1) + i * 4)
                        for back in (1, 2):
                            for c in (2 * p, 2 * p + 1):
                                u = ps[:, 2 * half + p, (c % 2) * SEQ:(c % 2 + 1) * SEQ - back]
                                if half == 0:
                                    dst = work[:, bass.ds(i * (FF_GROUP * SEQ) + c * SEQ + back, SEQ - back)]
                                else:
                                    dst = tmp[1][:, c * SEQ + back:(c + 1) * SEQ]
                                last = stt(dst, u, conv_group[:, 2 - back, half, c:c + 1], dst, ALU.mult, ALU.add)
                            link(last)
                        if p == 1:
                            dve.sem_inc((gate_conv, up_taken)[half], 1)
                    elif p == 2:
                        if half == 0:
                            dve.wait_ge(gate_sigmoid, layered(l, FF_GROUPS, 1) + i)
                        link(tt(group, group, tmp[half], ALU.mult))
                    else:
                        set_taps(1 - half, i + half)

                dve.wait_ge(conv_copied, layered(l, 1, 1))
                set_taps(0, 0)
                dve.wait_ge(ple_vec_loaded, layered(l, 16, 16))

                def finish_ple(n):
                    m, cols = n // 2, slice((n % 2) * 1024, (n % 2 + 1) * 1024)
                    dve.wait_ge(ple_sigmoid, layered(l, 4, n + 1))
                    link(tt(ple[:, m, cols], ple[:, m, cols], gate_sums[:, n, :], ALU.mult))
                    link(stt(xt[:, m, cols], xt[:, m, cols], ALPHA, ple[:, m, cols], ALU.mult, ALU.add))

                for n in range(4):
                    cols = slice((n % 2) * 1024, (n % 2 + 1) * 1024)
                    bank_made(l, UP_AT, 1, 2 * n + 1)
                    tt(gate_sums[:, n, :].rearrange("p (b c) -> p b c", b=2), ps[:, 2 * n:2 * n + 2, :],
                       vec[:, 0, cols].rearrange("p (b c) -> p b c", b=2), ALU.add).then_inc(ple_sums, 1)
                for n in range(4):
                    split(l, UP_AT + n + 1)
                    finish_ple(n)
                stand_alone(dve)
                with link.loop(FF_GROUPS - 1, UP_LINKS) as i:
                    for j in range(UP_BODY):
                        split(l, UP_AT + 4 + j + 1, i, UP_BODY)
                        convolve(j // 4, j % 4, i)

                def down_step(j, i):
                    split(l, DOWN_AT + j, i, 4)
                    dve.wait_ge(g_hi, layered(l, KFF, j + 1) + i * 4)
                    tt(xT_lo[:, j % 4, :], work[:, bass.ds(i * (4 * SEQ) + j * SEQ, SEQ)],
                       xT_hi[:, j % 4, :].bitcast(F32), ALU.subtract).then_inc(g_split, 1)

                for j in range(4):
                    if j < 3:
                        split(l, DOWN_AT - 4 + j + 1)
                    else:
                        down_step(0, 0)
                    convolve(0, j, FF_GROUPS - 1)

                for j in range(4):
                    if j == 0:
                        convolve(1, 0, FF_GROUPS - 1)
                        convolve(1, 1, FF_GROUPS - 1)
                    down_step(j + 1, 0)
                    if j == 1:
                        convolve(1, 2, FF_GROUPS - 1)
                stand_alone(dve)
                with dve.Fori(1, KFF // 4 - 1) as i:
                    for j in range(4):
                        down_step(j + 1, i)
                for j in range(3):
                    down_step(j + 1, KFF // 4 - 1)
                add_and_norm(l, PANELS, 2, 1.0, 1)

        @block.tensor
        def _(pe):
            mm = nc.tensor.matmul

            def panel(l, at, i, step, products, show=False):
                pe.wait_ge(panels_split, layered(l, PANELS, at + 1 + RAW_SLOTS) + i * step)
                for at_product, (bank, hi, lo, x_hi, x_lo, first, last, flip, wait) in enumerate(products):
                    if wait:
                        pe.wait_ge(*wait)
                    pairs = ((x_hi, lo), (x_hi, hi), (x_lo, hi))
                    for n, (x, w) in enumerate(pairs):
                        lhs, rhs = (w, x) if flip else (x, w)
                        done = mm(bank, lhs, rhs, start=first and n == 0, stop=last and n == 2,
                                  skip_group_check=flip)
                    if show and last and at_product < len(products) - 1:
                        done.then_inc(banks_made, 1)
                done.then_inc(panels_used, 1)

            def tokens_by_columns(s, k_chunks, width, x_slots, banks, first, last, xh=xT_hi, xl=xT_lo,
                                  order=None, waits={}):
                order = order or [(m, n) for m in range(M) for n in range((width + BANK - 1) // BANK)]
                found = []
                for k in range(k_chunks):
                    for m, n in order:
                        lo, hi = k * width + n * BANK, k * width + min(width, (n + 1) * BANK)
                        x = (slice(None), x_slots[k], slice(m * P, (m + 1) * P))
                        found.append((banks(m, n)[:, 0:hi - lo], w_hi[:, s, lo:hi], w_lo[:, s, lo:hi], xh[x], xl[x],
                                      first and k == 0, last and k == k_chunks - 1, False, waits.get((m, n))))
                return found

            def transpose(dst, src):
                return nc.tensor.transpose(dst, src, ident[:, :])

            def transpose_x(l, norm):
                for b in range(XT_BANKS):
                    if b == 0:
                        pe.wait_ge(left_normed, layered(l, 2 * M, M * (norm + 1)))
                    if b == 4:
                        for normed in right_normed:
                            pe.wait_ge(normed, layered(l, 2, norm + 1))
                    if norm == 1:
                        pe.wait_ge(ple_copied, layered(l, 8, b + 1))
                    for k in (2 * b, 2 * b + 1):
                        for m in range(M):
                            col = (k % 2) * SEQ + m * P
                            last = transpose(ps[:, XT_PSUM[norm][b], col:col + P], xt[:, m, k * P:(k + 1) * P])
                    last.then_inc(transposed, 1)

            def wide(l, at, slot, first, last, i=0, step=0, xh=xT_hi, xl=xT_lo, order=None, waits={}, show=False):
                panel(l, at, i, step,
                      tokens_by_columns(at % SPLIT_SLOTS, 1, D_MODEL, [slot], lambda m, n: ps[:, 4 * m + n, :],
                                        first, last, xh, xl, order, waits), show)

            pe.sem_inc(panels_used, SPLIT_SLOTS)
            pe.wait_ge(ident_loaded, 16)
            for loaded in x_loaded:
                pe.wait_ge(loaded, 16)

            with pe.Fori(0, DEPTH) as l:
                def project_kv(n):
                    pe.wait_ge(xT_lo_done, layered(l, T_BANKS, 4 if n == 0 else XT_BANKS))
                    panel(l, KV_AT + n, 0, 0,
                          tokens_by_columns((KV_AT + n) % SPLIT_SLOTS, 8, 256, range(8 * n, 8 * n + 8),
                                            lambda m, n: ps[:, m, :], n == 0, n == 1))

                transpose_x(l, 0)
                project_kv(0)
                project_kv(1)
                pe.wait_ge(p_loaded, layered(l, 16, 16))
                for k in range(PLE_PANELS):
                    for m in range(M):
                        last = transpose(ps[:, P_PSUM, k * SEQ + m * P:k * SEQ + (m + 1) * P], p_tok[:, m, k * P:(k + 1) * P])
                last.then_inc(transposed, 1)


                def transpose_aqk(n):
                    pe.wait_ge(att_rotated, layered(l, M, M))
                    if n == 4:
                        pe.wait_ge(aqk_copied, layered(l, AQK_BANKS, 3))
                    for c in range(2):
                        for m in range(M):
                            src = k_twice[:, m, c, :, :].rearrange("p e d -> p (e d)") if n == 0 else \
                                proj[:, m, AQ + (2 * n - 2 + c) * P:AQ + (2 * n - 1 + c) * P]
                            last = transpose(ps[:, AQK_PSUM[n], c * SEQ + m * P:c * SEQ + (m + 1) * P], src)
                    last.then_inc(aqk_transposed, 1)

                def scores(n):
                    m, quad, keys = n // 4, n % 4, P * (1 + n // 4)
                    pe.wait_ge(aqk_copied, layered(l, AQK_BANKS, min(n, 3) + 2))
                    if n:
                        pe.wait_ge(max_done, layered(l, UNITS, n))
                    for c in range(2):
                        for e in range(2):
                            half = slice(64 * e, 64 * e + 64)
                            last = mm(ps[:, 4 + e, c * 256:c * 256 + keys],
                                      aqT[half, 2 * quad + c, m * P:(m + 1) * P],
                                      akT[half, quad // 2, 0:keys], start=True, stop=True)
                    last.then_inc(scores_done, 1)

                def transpose_probs(n):
                    u, kc = n % 2, 1 + n // 4
                    pe.wait_ge(probs_done, layered(l, UNITS, n + 1))
                    if n == 0:
                        pe.wait_ge(aqk_copied, layered(l, AQK_BANKS, AQK_BANKS))
                    else:
                        pe.wait_ge(att_copied, layered(l, UNITS, n))
                    for h in range(4):
                        for k in range(kc):
                            col = (h % 2) * 256 + k * P
                            last = transpose(ps[:, 6 + h // 2, col:col + P], probs[u][:, h, k * P:(k + 1) * P])
                    last.then_inc(probsT_done, 1)

                def attend(n):
                    quad, u, kc = n % 4, n % 2, 1 + n // 4
                    pe.wait_ge(probsT_copied, layered(l, 2 * UNITS, 2 * n + 2))
                    v = slice(AV + (quad // 2) * ATT_DIM, AV + (quad // 2 + 1) * ATT_DIM)
                    for c in range(2):
                        for e in range(2):
                            for k in range(kc):
                                last = mm(ps[64 * e:64 * e + 64, 6, c * P:(c + 1) * P], proj[:, k, v],
                                          probsT[u][:, 2 * c + e, k * P:(k + 1) * P], start=k == 0, stop=k == kc - 1)
                    last.then_inc(att_done, 1)

                def transpose_rqk(n):
                    order = RQK_ORDER.index(n)
                    pe.wait_ge(ret_rotated, layered(l, 2, 1 + n // 4))
                    pe.wait_ge(max_done, layered(l, UNITS, UNITS))
                    if order >= 2:
                        pe.wait_ge(rqk_copied, layered(l, 8, order - 1))
                    for c in range(2):
                        for m in range(M):
                            last = transpose(ps[:, 4 + n % 2, c * SEQ + m * P:c * SEQ + (m + 1) * P],
                                             proj[:, m, (2 * n + c) * P:(2 * n + c + 1) * P])
                    last.then_inc(rqk_transposed, 1)

                def ret_scores(h):
                    pe.wait_ge(rqk_copied, layered(l, 8, 8))
                    if h < 2:
                        pe.wait_ge(att_copied, layered(l, UNITS, UNITS))
                    else:
                        pe.wait_ge(ret_scores_masked, layered(l, RET_HEADS, h - 1))
                    for col, j, i in ((0, 0, 0), (P, 1, 1), (2 * P, 0, 1)):
                        for k in range(2):
                            last = mm(ps[:, 6 + h % 2, col:col + P], rkT[:, 2 * h + k, j * P:(j + 1) * P],
                                      rqT[:, 2 * h + k, i * P:(i + 1) * P], start=k == 0, stop=k == 1)
                    last.then_inc(ret_scores_done, 1)

                def ret_attend(h, v_made):
                    pe.wait_ge(proj_copied, layered(l, COPIES, M * (1 + v_made // HALF_PANELS) + 1))
                    pe.wait_ge(ret_scores_masked, layered(l, RET_HEADS, h + 1 if h < 2 else RET_HEADS))
                    s, cols = scoresT[h], slice(RV + h * RET_DIM, RV + (h + 1) * RET_DIM)
                    y = ps[:, 4 + h, :].rearrange("p (m c) -> p m c", m=M)
                    mm(y[:, 0, :], s[:, 0:P], proj[:, 0, cols], start=True, stop=True)
                    mm(y[:, 1, :], s[:, 2 * P:3 * P], proj[:, 0, cols], start=True, stop=False)
                    mm(y[:, 1, :], s[:, P:2 * P], proj[:, 1, cols], start=False, stop=True).then_inc(ret_done, 1)

                def transpose_ret(pair):
                    pe.wait_ge(ret_gated[pair], layered(l, 1, 1))
                    pe.wait_ge(proj_copied, layered(l, COPIES, COPIES + 1))
                    pe.wait_ge(ret_copied, layered(l, RET_HEADS, 2 * pair + 2))
                    for b in (2 * pair, 2 * pair + 1):
                        for c in range(2):
                            for m in range(M):
                                last = transpose(ps[:, RET_PSUM[b], c * SEQ + m * P:c * SEQ + (m + 1) * P],
                                                 ret_y[:, m, (2 * b + c) * P:(2 * b + c + 1) * P])
                        last.then_inc(ret_transposed, 1)

                for s in range(STEPS):
                    at = IN_AT + s
                    if s < RV_MADE:
                        q, j = s // HALF_PANELS, s % HALF_PANELS
                        if j == 0:
                            pe.wait_ge(proj_copied, layered(l, COPIES, M * q + 1))
                        panel(l, at, 0, 0,
                              tokens_by_columns(at % SPLIT_SLOTS, 4, 512, range(4 * j, 4 * j + 4),
                                                lambda m, n: ps[:, 2 - 2 * (q % 2) + m, :], j == 0, j == 3))
                    else:
                        j, right = (s - RV_MADE) % 4, (s - RV_MADE) // 4
                        order, waits = None, {}
                        if not right:
                            pe.wait_ge(att_lo, layered(l, 4, j + 1))
                            pe.wait_ge(ret_copied, layered(l, RET_HEADS, 2))
                            if j == 0:
                                order = [(1, 0), (1, 1), (0, 0), (0, 1)]
                                waits = {(0, 0): (proj_copied, layered(l, COPIES, COPIES + 1))}
                        elif j == 0:
                            waits = {(0, 0): (ret_lo, layered(l, 4, 2)), (1, 0): (ret_lo, layered(l, 4, 4))}
                        panel(l, at, 0, 0,
                              tokens_by_columns(at % SPLIT_SLOTS, 2, 1024, (8 + 2 * j, 9 + 2 * j),
                                                lambda m, n: ps[:, 4 * m + 2 * right + n, :], j == 0, False,
                                                order=order, waits=waits))
                    for n in AQK_TRANSPOSE.get(s, ()):
                        transpose_aqk(n)
                    if (n := unit(s, SCORES)) is not None:
                        scores(n)
                    if (n := unit(s, ATTEND)) is not None:
                        attend(n)
                    if (n := unit(s, TRANSPOSE_P)) is not None:
                        transpose_probs(n)
                    for n in RQK_TRANSPOSE.get(s, ()):
                        transpose_rqk(n)
                    if 0 <= s - RET_SCORES < RET_HEADS:
                        ret_scores(s - RET_SCORES)
                    for pair in range(2):
                        if s == RET_PV[pair]:
                            ret_attend(2 * pair, s)
                            ret_attend(2 * pair + 1, s)
                    if s == RV_MADE + 1:
                        transpose_ret(0)
                    if s == RV_MADE + 3:
                        transpose_ret(1)

                for n in range(8, OUT_PANELS):
                    wide(l, OUT_AT + n, n - 8, False, n == OUT_PANELS - 1, show=True)

                pe.wait_ge(conv_loaded, layered(l, 64, 64))
                pe.wait_ge(sums_taken, layered(l, 16, 1))
                for k in range(4):
                    last = nc.tensor.transpose(ps[:, 0, k * 2 * KFF:(k + 1) * 2 * KFF], conv_rows[0:2 * KFF, k, :],
                                               ident[0:2 * KFF, 0:2 * KFF])
                last.then_inc(conv_transposed, 1)

                order = [(b // 4, b % 4) for b in PLE_BANKS]
                waits = {(b // 4, b % 4): (sums_taken, layered(l, 16, b + 1)) for b in PLE_BANKS if b}
                waits[0, 0] = (conv_copied, layered(l, 1, 1))
                for n in range(PLE_PANELS):
                    wide(l, PLE_AT + n, n, n == 0, n == PLE_PANELS - 1, xh=pT_hi, xl=pT_lo, order=order,
                         waits=waits if n == 0 else {})

                transpose_x(l, 1)
                waits = {(b // 4, b % 4): (xT_lo_done, layered(l, T_BANKS, XT_BANKS + 2 + n))
                         for n, b in enumerate(PLE_BANKS)}
                for n in range(GATE_PANELS):
                    wide(l, GATE_AT + n, n, n == 0, n == GATE_PANELS - 1,
                         order=order if n == 0 else None, waits=waits if n == 0 else {}, show=True)

                with pe.Fori(0, FF_GROUPS) as i:
                    for half in range(2):
                        pe.wait_ge(ple_sums, layered(l, 4, half + 1))
                        pe.wait_ge((gate_conv, up_taken)[half], layered(l, FF_GROUPS, 1) + i)
                        for j in range(4):
                            at = UP_AT + 4 * half + j
                            s = at % SPLIT_SLOTS
                            products = []
                            for k in range(4):
                                for c in range(FF_GROUP):
                                    w = slice(k * 512 + c * P, k * 512 + (c + 1) * P)
                                    products.append((ps[:, 2 * half + c // 2, (c % 2) * SEQ:(c % 2 + 1) * SEQ],
                                                     w_hi[:, s, w], w_lo[:, s, w],
                                                     xT_hi[:, 4 * j + k, :], xT_lo[:, 4 * j + k, :],
                                                     j == 0 and k == 0 and c % 2 == 0, j == 3 and k == 3, True, None))
                            panel(l, at, i, UP_BODY, products)

                pe.wait_ge(ple_sums, layered(l, 4, 4))
                order = [(1, n) for n in range(4)] + [(0, n) for n in range(4)]
                waits = {(0, 0): (gate_conv, layered(l, FF_GROUPS, FF_GROUPS + 1)),
                         (0, 2): (up_taken, layered(l, FF_GROUPS, FF_GROUPS + 1))}

                def down(j, i, first=False, last=False, order=None, waits={}):
                    pe.wait_ge(g_split, layered(l, KFF, j + 1) + i * 4)
                    wide(l, DOWN_AT + j, j, first, last, i=i, step=4, order=order, waits=waits, show=True)

                down(0, 0, first=True, order=order, waits=waits)
                for j in range(1, 4):
                    down(j, 0)
                with pe.Fori(1, KFF // 4 - 1) as i:
                    for j in range(4):
                        down(j, i)
                for j in range(4):
                    down(j, KFF // 4 - 1, last=j == 3)


UP_LINKS = 2 * (2 * 2 + 1 + 1)
LINKS = 4 + UNITS * 5 + 2 * RET_HEADS * M + 5 + 2 * (3 * M + 1) + 1 + 8 + FF_GROUPS * UP_LINKS - 1
POOL_LINKS = 4 + 2 * M * 4 + 2 + 1 + 2


def constants():
    f = np.float32
    ret = f(1.0) / np.power(f(10000.0), np.linspace(0.0, 1.0, RET_DIM // 2, dtype=f))
    att = np.power(f(10000.0), -np.arange(0, ATT_DIM, 2, dtype=f) / f(ATT_DIM))
    i = np.arange(P)
    later = i[:, None] >= i[None, :]
    band = np.where(np.concatenate([~later, later], 1), 0.0, MASKED)
    gamma = np.log1p(-np.exp2(-5.0 - np.arange(RET_HEADS)))
    t = (np.arange(SEQ) - SEQ // 2)[:, None]
    decay = np.concatenate([np.exp(gamma * t), np.exp(-gamma * t) * RET_DIM ** -0.5], 1)
    return {
        "c_freq": np.concatenate([ret, att])[None, :].astype(f),
        "c_ident": np.eye(P, dtype=f),
        "c_band": band.astype(f),
        "c_causal": (i[:, None] <= i[None, :]).astype(f),
        "c_decay": np.ascontiguousarray(decay.reshape(M, P, 2 * RET_HEADS).transpose(1, 0, 2)).astype(f),
    }


def kernel(**inputs):
    import concourse.bacc as bacc
    from concourse.bass_utils import run_bass_kernel_spmd

    nc = bacc.Bacc("TRN2", target_bir_lowering=False, num_devices=1)
    arrays, aps = {}, {}
    for name, value in [*inputs.items(), *constants().items()]:
        value = np.ascontiguousarray(value)
        arrays[f"in_{name}"] = value
        aps[name] = nc.dram_tensor(f"in_{name}", value.shape, mybir.dt.from_np(value.dtype), kind="ExternalInput").ap()
    out = nc.dram_tensor("out_x", (1, SEQ, D_MODEL), F32, kind="ExternalOutput").ap()
    build(nc, aps, out)
    result = run_bass_kernel_spmd(nc, [arrays], core_ids=[0])
    return result.results[0]["out_x"]
```
